# Optimizing a Trainium2 kernel written in Bass

```python
import jax, jax.numpy as jnp
from jax import lax
import numpy as np

D_MODEL = 1024
BATCH = 1
SEQ = 256
DEPTH = 1
DEC_BATCH = 1
DEC_SEQ = 1024
PAST_LEN = 256

GRID_W = 64
D_ATT = 512
N_HEADS_ATT = 8
HEAD_DIM = 64
WIN_H = 8
WIN_W = 16
BAND_W = 2 * WIN_W
ATT_QBLOCK = 128
ATT_SCALE = HEAD_DIM ** -0.5
NEG_INF = -1e30
D_RG = 512
N_RG_BLOCKS = 8
RG_BLOCK = D_RG // N_RG_BLOCKS
CONV_W = 4
CONV_PAD_L = 2
CONV_PAD_R = 1
RG_C = 8.0
D_IN = 3 * D_ATT + 2 * D_RG
D_MIX = D_ATT + D_RG
N_KEYS = 128
N_EXPERTS = N_KEYS * N_KEYS
PEER_HEADS = 8
PEER_D_KEY = 256
PEER_D_HALF = PEER_D_KEY // 2
PEER_TOPK = 16
PEER_CHUNK = 128
RMS_EPS = 1e-6

kernel_name = "hybrid_natten_rglru_peer_diffusion_step"

def rmsnorm(x, w):
    xf = x.astype(jnp.float32)
    y = xf * lax.rsqrt(jnp.mean(xf * xf, axis=-1, keepdims=True) + RMS_EPS)
    return (y * w.astype(jnp.float32)).astype(x.dtype)

def adaln_params(cvec, w_mod, b_mod):
    m = jax.nn.silu(cvec) @ w_mod + b_mod
    return m.reshape(cvec.shape[0], 6, D_MODEL)

def modulate(h, shift, scale):
    return h * (1 + scale[:, None, :]) + shift[:, None, :]

def mixing_inputs(x, mod, norm_w, w_in):
    B, T, _ = x.shape
    h = modulate(rmsnorm(x, norm_w), mod[:, 0], mod[:, 1])
    proj = h @ w_in
    q, k, v, xr, yr = jnp.split(proj, [D_ATT, 2 * D_ATT, 3 * D_ATT, 3 * D_ATT + D_RG], axis=-1)
    heads = lambda t: t.reshape(B, T, N_HEADS_ATT, HEAD_DIM)
    return heads(q), heads(k), heads(v), xr, yr

def context_attention(q, k, v):
    B, L, H, Dh = q.shape
    nb = L // ATT_QBLOCK
    q_blocks = jnp.moveaxis(q.reshape(B, nb, ATT_QBLOCK, H, Dh), 1, 0)

    def one_block(q_b):
        s = jnp.einsum('bqhd,bkhd->bhqk', q_b, k).astype(jnp.float32) * ATT_SCALE
        p = jax.nn.softmax(s, axis=-1).astype(v.dtype)
        return jnp.einsum('bhqk,bkhd->bqhd', p, v)

    out = lax.map(one_block, q_blocks)
    return jnp.moveaxis(out, 0, 1).reshape(B, L, H * Dh)

def neighbourhood_attention(q, k, v, k_ctx, v_ctx, rpb):
    B, T, H, Dh = q.shape
    rows = T // GRID_W
    kh = min(WIN_H, rows)
    ncb = GRID_W // WIN_W
    r = jnp.arange(rows)
    row_idx = jnp.clip(r - kh // 2, 0, rows - kh)[:, None] + jnp.arange(kh)[None, :]
    row_bias_idx = row_idx - r[:, None] + (WIN_H - 1)
    cb = jnp.arange(ncb) * WIN_W
    qcol = cb[:, None] + jnp.arange(WIN_W)[None, :]
    band_idx = jnp.clip(cb - WIN_W // 2, 0, GRID_W - BAND_W)[:, None] + jnp.arange(BAND_W)[None, :]
    col_start = jnp.clip(qcol - WIN_W // 2, 0, GRID_W - WIN_W)
    kcol = band_idx[:, None, :]
    col_valid = (kcol >= col_start[:, :, None]) & (kcol < col_start[:, :, None] + WIN_W)
    col_bias_idx = jnp.clip(kcol - qcol[:, :, None] + (WIN_W - 1), 0, 2 * WIN_W - 2)
    k_grid = k.reshape(B, rows, GRID_W, H, Dh)
    v_grid = v.reshape(B, rows, GRID_W, H, Dh)
    q_rows = jnp.moveaxis(q.reshape(B, rows, ncb, WIN_W, H, Dh), 1, 0)
    n_loc = kh * BAND_W

    def one_row(args):
        q_r, ridx, rbias = args
        gi_r = ridx[None, :, None]
        gi_c = band_idx[:, None, :]
        k_b = k_grid[:, gi_r, gi_c]
        v_b = v_grid[:, gi_r, gi_c]
        s_loc = jnp.einsum('bcqhd,bcjwhd->bhcqjw', q_r, k_b).astype(jnp.float32) * ATT_SCALE
        bias = rpb[:, rbias[None, None, :, None], col_bias_idx[:, :, None, :]]
        s_loc = jnp.where(col_valid[:, :, None, :], s_loc + bias.astype(jnp.float32), NEG_INF)
        s_ctx = jnp.einsum('bcqhd,blhd->bhcql', q_r, k_ctx).astype(jnp.float32) * ATT_SCALE
        s = jnp.concatenate([s_loc.reshape(B, H, ncb, WIN_W, n_loc), s_ctx], axis=-1)
        p = jax.nn.softmax(s, axis=-1).astype(v.dtype)
        p_loc = p[..., :n_loc].reshape(B, H, ncb, WIN_W, kh, BAND_W)
        return (jnp.einsum('bhcqjw,bcjwhd->bcqhd', p_loc, v_b)
                + jnp.einsum('bhcql,blhd->bcqhd', p[..., n_loc:], v_ctx))

    out = lax.map(one_row, (q_rows, row_idx, row_bias_idx))
    return jnp.moveaxis(out, 0, 1).reshape(B, T, H * Dh)

def centred_depthwise_conv(x, w, b):
    T = x.shape[1]
    xp = jnp.pad(x, ((0, 0), (CONV_PAD_L, CONV_PAD_R), (0, 0)))
    out = xp[:, 0:T] * w[0] + b
    for i in range(1, CONV_W):
        out = out + xp[:, i:i + T] * w[i]
    return out

def _lin_combine(left, right):
    a_l, b_l = left
    a_r, b_r = right
    return (a_l * a_r, a_r * b_l + b_r)

def rglru_direction(xc, w_a, b_a, w_i, b_i, lam, h0, reverse):
    B, T, _ = xc.shape
    xb = xc.reshape(B, T, N_RG_BLOCKS, RG_BLOCK)
    r = jax.nn.sigmoid(jnp.einsum('btnc,ncd->btnd', xb, w_a.astype(jnp.float32)).reshape(B, T, D_RG)
                       + b_a.astype(jnp.float32))
    i = jax.nn.sigmoid(jnp.einsum('btnc,ncd->btnd', xb, w_i.astype(jnp.float32)).reshape(B, T, D_RG)
                       + b_i.astype(jnp.float32))
    log_a = RG_C * r * jax.nn.log_sigmoid(lam.astype(jnp.float32))
    a = jnp.exp(log_a)
    b = jnp.sqrt(-jnp.expm1(2 * log_a)) * (i * xc)
    edge = -1 if reverse else 0
    b = b.at[:, edge].add(a[:, edge] * h0.astype(jnp.float32))
    _, h = lax.associative_scan(_lin_combine, (a, b), reverse=reverse, axis=1)
    return h

def bidir_rglru(xr, yr, h0, conv_w, conv_b, w_a, b_a, w_i, b_i, lam):
    xc = centred_depthwise_conv(xr, conv_w, conv_b).astype(jnp.float32)
    h_f = rglru_direction(xc, w_a[0], b_a[0], w_i[0], b_i[0], lam[0], h0[:, 0], False)
    h_b = rglru_direction(xc, w_a[1], b_a[1], w_i[1], b_i[1], lam[1], h0[:, 1], True)
    y = ((h_f + h_b) * jax.nn.gelu(yr.astype(jnp.float32), approximate=True)).astype(xr.dtype)
    return y, h_f, h_b

def mixer_residual(x, mod, att, rg_out, w_out):
    out = jnp.concatenate([att, rg_out], axis=-1) @ w_out
    return x + mod[:, 2][:, None, :] * out

def peer_ffn(x, w_q, sub_keys, u, v):
    N = x.shape[0]
    q = (x @ w_q).reshape(N, PEER_HEADS, 2, PEER_D_HALF)
    s = jnp.einsum('nhpd,pkd->nhpk', q, sub_keys).astype(jnp.float32)
    s_top, i_top = lax.top_k(s, PEER_TOPK)
    cand = (s_top[:, :, 0, :, None] + s_top[:, :, 1, None, :]).reshape(N, PEER_HEADS, PEER_TOPK * PEER_TOPK)
    best, best_pos = lax.top_k(cand, PEER_TOPK)
    idx1 = jnp.take_along_axis(i_top[:, :, 0], best_pos // PEER_TOPK, axis=-1)
    idx2 = jnp.take_along_axis(i_top[:, :, 1], best_pos % PEER_TOPK, axis=-1)
    expert = (idx1 * N_KEYS + idx2).reshape(N, PEER_HEADS * PEER_TOPK)
    g = jax.nn.softmax(best, axis=-1).astype(x.dtype).reshape(N, PEER_HEADS * PEER_TOPK)
    nc = N // PEER_CHUNK

    def one_chunk(args):
        x_c, e_c, g_c = args
        act = jax.nn.gelu(jnp.einsum('cd,ced->ce', x_c, u[e_c]), approximate=False)
        return jnp.einsum('ce,ced->cd', g_c * act, v[e_c])

    out = lax.map(one_chunk, (x.reshape(nc, PEER_CHUNK, D_MODEL),
                              expert.reshape(nc, PEER_CHUNK, -1), g.reshape(nc, PEER_CHUNK, -1)))
    return out.reshape(N, D_MODEL)

def ffn_sublayer(x, mod, norm_w, w_q, sub_keys, u, v):
    B, T, D = x.shape
    h = modulate(rmsnorm(x, norm_w), mod[:, 3], mod[:, 4])
    out = peer_ffn(h.reshape(B * T, D), w_q, sub_keys, u, v).reshape(B, T, D)
    return x + mod[:, 5][:, None, :] * out

def setup_inputs(seed: int = 0) -> dict:
    key = jax.random.key(seed)
    ks = jax.random.split(key, 26)
    nrm = lambda k, shape, s: jax.random.normal(k, shape, jnp.float32) * s
    lam_u = jax.random.uniform(ks[18], (DEPTH, 2, D_RG), jnp.float32, minval=0.9, maxval=0.999)
    return {
        "x_prompt": nrm(ks[0], (BATCH, SEQ, D_MODEL), 1.0),
        "x_sample": nrm(ks[1], (DEC_BATCH, DEC_SEQ, D_MODEL), 1.0),
        "c": nrm(ks[2], (DEC_BATCH, D_MODEL), 1.0),
        "cache_k": nrm(ks[3], (DEC_BATCH, DEPTH, PAST_LEN, N_HEADS_ATT, HEAD_DIM), 1.0),
        "cache_v": nrm(ks[4], (DEC_BATCH, DEPTH, PAST_LEN, N_HEADS_ATT, HEAD_DIM), 1.0),
        "state_rglru": nrm(ks[5], (DEC_BATCH, DEPTH, 2, D_RG), 0.5),
        "c_ctx": nrm(ks[6], (D_MODEL,), 1.0),
        "w_mod": nrm(ks[7], (DEPTH, D_MODEL, 6 * D_MODEL), 0.5 * D_MODEL ** -0.5),
        "b_mod": nrm(ks[8], (DEPTH, 6 * D_MODEL), 0.02),
        "norm_mix_w": 1.0 + nrm(ks[9], (DEPTH, D_MODEL), 0.02),
        "w_in": nrm(ks[10], (DEPTH, D_MODEL, D_IN), D_MODEL ** -0.5),
        "rpb": nrm(ks[11], (DEPTH, N_HEADS_ATT, 2 * WIN_H - 1, 2 * WIN_W - 1), 0.1),
        "conv_w": nrm(ks[12], (DEPTH, CONV_W, D_RG), CONV_W ** -0.5),
        "conv_b": nrm(ks[13], (DEPTH, D_RG), 0.02),
        "rg_w_a": nrm(ks[14], (DEPTH, 2, N_RG_BLOCKS, RG_BLOCK, RG_BLOCK), RG_BLOCK ** -0.5),
        "rg_b_a": nrm(ks[15], (DEPTH, 2, D_RG), 0.02),
        "rg_w_i": nrm(ks[16], (DEPTH, 2, N_RG_BLOCKS, RG_BLOCK, RG_BLOCK), RG_BLOCK ** -0.5),
        "rg_b_i": nrm(ks[17], (DEPTH, 2, D_RG), 0.02),
        "rg_lambda": jnp.log(lam_u) - jnp.log1p(-lam_u),
        "w_out": nrm(ks[19], (DEPTH, D_MIX, D_MODEL), D_MIX ** -0.5),
        "norm_ffn_w": 1.0 + nrm(ks[20], (DEPTH, D_MODEL), 0.02),
        "peer_w_q": nrm(ks[21], (DEPTH, D_MODEL, PEER_HEADS * PEER_D_KEY), D_MODEL ** -0.5),
        "peer_sub_keys": nrm(ks[22], (DEPTH, 2, N_KEYS, PEER_D_HALF), PEER_D_HALF ** -0.5),
        "peer_u": nrm(ks[23], (DEPTH, N_EXPERTS, D_MODEL), D_MODEL ** -0.5),
        "peer_v": nrm(ks[24], (DEPTH, N_EXPERTS, D_MODEL), 0.5),
        "norm_f_w": 1.0 + nrm(ks[25], (D_MODEL,), 0.02),
    }

def reference(x_prompt, x_sample, c, cache_k, cache_v, state_rglru, c_ctx, w_mod, b_mod, norm_mix_w, w_in,
              rpb, conv_w, conv_b, rg_w_a, rg_b_a, rg_w_i, rg_b_i, rg_lambda, w_out, norm_ffn_w,
              peer_w_q, peer_sub_keys, peer_u, peer_v, norm_f_w):
    xp = x_prompt
    xs = x_sample
    new_k, new_v, new_h = [], [], []
    for l in range(DEPTH):
        rg = (conv_w[l], conv_b[l], rg_w_a[l], rg_b_a[l], rg_w_i[l], rg_b_i[l], rg_lambda[l])
        peer = (peer_w_q[l], peer_sub_keys[l], peer_u[l], peer_v[l])
        mod_p = adaln_params(c_ctx[None, :], w_mod[l], b_mod[l])
        q, k, v, xr, yr = mixing_inputs(xp, mod_p, norm_mix_w[l], w_in[l])
        att = context_attention(q, k, v)
        h0 = jnp.zeros((xp.shape[0], 2, D_RG), jnp.float32)
        rg_out, h_f, h_b = bidir_rglru(xr, yr, h0, *rg)
        xp = mixer_residual(xp, mod_p, att, rg_out, w_out[l])
        xp = ffn_sublayer(xp, mod_p, norm_ffn_w[l], *peer)
        new_k.append(k)
        new_v.append(v)
        new_h.append(jnp.stack([h_f[:, -1], h_b[:, 0]], axis=1).astype(x_prompt.dtype))
        mod_s = adaln_params(c, w_mod[l], b_mod[l])
        q, k, v, xr, yr = mixing_inputs(xs, mod_s, norm_mix_w[l], w_in[l])
        att = neighbourhood_attention(q, k, v, cache_k[:, l], cache_v[:, l], rpb[l])
        rg_out, _, _ = bidir_rglru(xr, yr, state_rglru[:, l], *rg)
        xs = mixer_residual(xs, mod_s, att, rg_out, w_out[l])
        xs = ffn_sublayer(xs, mod_s, norm_ffn_w[l], *peer)
    y_prompt = rmsnorm(xp, norm_f_w)
    y_sample = rmsnorm(xs, norm_f_w)
    new_cache_k = jnp.stack(new_k, axis=1)
    new_cache_v = jnp.stack(new_v, axis=1)
    new_state_rglru = jnp.stack(new_h, axis=1)
    return (y_prompt, y_sample, new_cache_k, new_cache_v, new_state_rglru)


_drawn_inputs = setup_inputs


def setup_inputs(seed=0):
    import zlib

    import numpy as np

    out = dict(_drawn_inputs(seed))
    spreads = {}
    factors = {'cache_k': 3.426,
     'cache_v': 2.861,
     'state_rglru': 6.07,
     'norm_mix_w': 2.859,
     'rpb': 8.0,
     'rg_b_a': 8.0,
     'rg_b_i': 6.837,
     'norm_ffn_w': 4.646,
     'norm_f_w': 2.803}
    for name, (base, spread) in spreads.items():
        noise = np.random.default_rng([zlib.crc32(name.encode()), seed]).standard_normal(out[name].shape)
        drawn = base * np.exp(spread * noise) if base else spread * noise
        out[name] = __import__('jax').numpy.asarray(drawn.astype(out[name].dtype))
    for name, factor in factors.items():
        out[name] = (out[name] * factor).astype(out[name].dtype)
    return out
```

```python
from contextlib import ExitStack

import numpy as np
import concourse.bass as bass
from concourse import mybir

FP32 = mybir.dt.float32
FP32R = mybir.dt.float32r
U32 = mybir.dt.uint32
I32 = mybir.dt.int32
ALU = mybir.AluOpType
ACT = mybir.ActivationFunctionType
AX = mybir.AxisListType.X

P = 128
D = 1024
KD = D // P
LATENT, CONTEXT = 1024, 256
T = LATENT + CONTEXT
TILES = T // P
LATENT_TILES = LATENT // P
DENSE_TILES, GATHER_TILES = 6, 4
CHUNKS = ((0, 512), (512, 512), (1024, 256))
SLAB = 512
HEADS, HD = 8, 64
GRID_W, WIN_H, WIN_W = 64, 8, 16
ROW_OFFSETS = 2 * WIN_H
PAST = 256
NEG = -1e30
LOWEST = -3e38
ATT_SCALE = HD ** -0.5
RG_TILES = 4
N_KEYS = 128
PEER_HEADS = 8
TOPK = 16
SLOTS = PEER_HEADS * TOPK
EPS = 1e-6
LATENT_COND, CONTEXT_COND = 0, 1


class Chain:

    def __init__(self, engine, semaphore):
        self.engine, self.semaphore, self.n = engine, semaphore, 0

    def step(self, instruction):
        instruction.then_inc(self.semaphore, 1)
        self.n += 1

    def wait(self):
        self.engine.wait_ge(self.semaphore, self.n)

    def link(self, instruction):
        self.step(instruction)
        self.wait()

    def reset(self):
        self.engine.sem_clear(self.semaphore)
        self.n = 0


class Scope:

    def __init__(self, nc, stage):
        self.nc, self.stage, self.stack, self.semaphores = nc, stage, ExitStack(), []

    def __enter__(self):
        return self

    def __exit__(self, *error):
        return self.stack.__exit__(*error)

    def sb(self, name, shape, dtype=FP32):
        return self.stack.enter_context(self.nc.sbuf_tensor(f"{self.stage}_{name}", shape, dtype))

    def psum(self, name, shape):
        return self.stack.enter_context(self.nc.psum_tensor(f"{self.stage}_{name}", shape, FP32))

    def sem(self, name):
        semaphore = self.stack.enter_context(self.nc.semaphore(f"{self.stage}_{name}"))
        self.semaphores.append(semaphore)
        return semaphore

    def block(self, clear=False):
        if clear:
            self.stack.callback(self.clear_semaphores)
        return self.stack.enter_context(self.nc.Block())

    def clear_semaphores(self):
        for semaphore in self.semaphores:
            self.nc.sync.sem_clear(semaphore)


def constants_and_modulation(nc, io, keep, scratch):
    RING = 3
    w_mod = io["w_mod"].rearrange("(j p) n -> p j n", p=P)
    with Scope(nc, "mod") as s:
        cond = s.sb("cond", [P, KD, 2])
        silu = s.sb("silu", [P, KD, 2])
        silu_rows = s.sb("silu_rows", [P, KD, 2, P])
        b_col = s.sb("b_col", [P, 6, KD])
        b_gate = s.sb("b_gate", [P, 2, D])
        norm_col = s.sb("norm_col", [P, 2, KD])
        slab = s.sb("slab", [P, RING, KD, SLAB])
        gate = s.sb("gate", [P, 2, 2, D])
        col_ps = [s.psum(f"col_ps{n}", [P, SLAB]) for n in range(2)]
        gate_ps = [s.psum(f"gate_ps{n}", [P, SLAB]) for n in range(4)]
        small_in = s.sem("small_in")
        slab_in = [s.sem(f"slab_in{n}") for n in range(RING)]
        slab_used = [s.sem(f"slab_used{n}") for n in range(RING)]
        silu_ready = s.sem("silu_ready")
        rows_ready = s.sem("rows_ready")
        cols_ready = s.sem("cols_ready")
        cols_taken = s.sem("cols_taken")
        gate_ready = s.sem("gate_ready")
        gate_taken = s.sem("gate_taken")
        own = s.sem("own_vector")
        own_pool = s.sem("own_pool")
        gate_out = s.sem("gate_out")
        block = s.block(clear=True)

        @block.sync
        def _(sp):
            sp.dma_start(cond[:, :, :], io["cond"]).then_inc(small_in, 16)
            sp.dma_start(b_col[:, :, :], io["b_mod_cols"]).then_inc(small_in, 16)
            sp.dma_start(norm_col[:, :, :], io["norm_cols"]).then_inc(small_in, 16)
            for g in range(2):
                at = (3 * g + 2) * D
                sp.dma_start(b_gate[:, g, :], io["b_mod"][at:at + D].partition_broadcast(P)).then_inc(small_in, 16)
            with sp.Fori(0, 2) as a:
                for n in range(6):
                    sp.wait_ge(slab_used[n % RING], 2 * a + n // RING)
                    sp.dma_start(slab[:, n % RING, :, :], w_mod[:, :, bass.ts(6 * a + n, SLAB)])\
                      .then_inc(slab_in[n % RING], 16)
            sp.wait_ge(gate_taken, 8)
            sp.dma_start(scratch["gate"].rearrange("g p c n -> p g c n"), gate[:, :, :, :]).then_inc(gate_out, 16)
            sp.wait_ge(gate_out, 16)

        @block.gpsimd
        def _(pool):
            c = Chain(pool, own_pool)
            c.link(nc.gpsimd.memset(keep["ident"][:, :], 0.0))
            c.link(nc.gpsimd.affine_select(out=keep["ident"][:, :], in_=keep["ident"][:, :],
                                           compare_op=ALU.not_equal, fill=1.0, base=0,
                                           pattern=[[-1, P]], channel_multiplier=1))
            c.link(nc.gpsimd.iota(keep["iota_int"][:, :], pattern=[[1, P]], base=0, channel_multiplier=0))
            c.link(nc.gpsimd.tensor_copy(keep["iota"][:, :], keep["iota_int"][:, :]))

        @block.scalar
        def _(act):
            act.wait_ge(small_in, 80)
            nc.scalar.activation(silu[:, :, :], cond[:, :, :], ACT.Silu).then_inc(silu_ready, 1)

        @block.tensor
        def _(pe):
            pe.wait_ge(silu_ready, 1)
            pe.wait_ge(rows_ready, 1)
            with pe.Fori(0, 2) as a:
                for n in range(6):
                    pe.wait_ge(slab_in[n % RING], 32 * a + 16 * (n // RING) + 16)
                    if n < 4:
                        if n >= 2:
                            pe.wait_ge(cols_taken, 4 * a + n - 1)
                        else:
                            pe.wait_ge(cols_taken, 4 * a)
                        for ct in range(4):
                            for k in range(KD):
                                last = nc.tensor.matmul(col_ps[n % 2][:, 2 * ct:2 * ct + 2], slab[:, n % RING, k, ct * P:(ct + 1) * P],
                                                        silu[:, k, :], start=(k == 0), stop=(k == KD - 1))
                        last.then_inc(cols_ready, 1)
                        pe.wait_ge(cols_ready, 4 * a + n + 1)
                    else:
                        if n == 4:
                            pe.wait_ge(gate_taken, 4 * a)
                        for cnd in range(2):
                            for k in range(KD):
                                last = nc.tensor.matmul(gate_ps[2 * (n - 4) + cnd][:, :], silu_rows[:, k, cnd, :],
                                                        slab[:, n % RING, k, :], start=(k == 0), stop=(k == KD - 1))
                            last.then_inc(gate_ready, 1)
                        pe.wait_ge(gate_ready, 4 * a + 2 * (n - 4) + 2)
                    pe.sem_inc(slab_used[n % RING], 1)

        @block.vector
        def _(dve):
            mod = keep["mod_cols"]
            dve.wait_ge(silu_ready, 1)
            nc.vector.tensor_copy(silu_rows[:, :, :, :],
                                  silu[:, :, :].unsqueeze(3).broadcast_to([P, KD, 2, P])).then_inc(rows_ready, 1)
            with dve.Fori(0, 2) as a:
                for n in range(4):
                    dve.wait_ge(cols_ready, 4 * a + n + 1)
                    nc.vector.tensor_tensor(
                        mod[:, 3 * a + n // 2, 4 * (n % 2):4 * (n % 2) + 4, :], col_ps[n % 2][:, 0:8].rearrange("p (c b) -> p c b", b=2),
                        b_col[:, 3 * a + n // 2, 4 * (n % 2):4 * (n % 2) + 4].unsqueeze(2).broadcast_to([P, 4, 2]),
                        ALU.add).then_inc(cols_taken, 1)
                for n in range(4):
                    dve.wait_ge(gate_ready, 4 * a + n + 1)
                    half = slice((n // 2) * SLAB, (n // 2 + 1) * SLAB)
                    nc.vector.tensor_tensor(gate[:, a, n % 2, half], gate_ps[n][:, :], b_gate[:, a, half],
                                            ALU.add).then_inc(gate_taken, 1)
            dve.wait_ge(cols_taken, 8)
            c = Chain(dve, own)
            for g in range(2):
                c.link(nc.vector.tensor_scalar_add(keep["factor"][:, g, :, :], mod[:, 3 * g + 1, :, :], 1.0))
                c.link(nc.vector.tensor_tensor(keep["factor"][:, g, :, :], keep["factor"][:, g, :, :],
                                               norm_col[:, g, :].unsqueeze(2).broadcast_to([P, KD, 2]), ALU.mult))


def input_norm(nc, io, keep, hT):
    with Scope(nc, "norm") as s:
        x = s.sb("x", [P, 2, D])
        xn = s.sb("xn", [P, 2, D])
        square = s.sb("square", [P, 2, D])
        total = s.sb("total", [P, 2])
        rstd = s.sb("rstd", [P, 2])
        eps = s.sb("eps", [P, 1])
        ps = [s.psum(f"ps{n}", [P, KD, P]) for n in range(2)]
        x_in = [s.sem(f"x_in{n}") for n in range(2)]
        eps_ready = s.sem("eps_ready")
        root_ready = s.sem("root_ready")
        rstd_ready = s.sem("rstd_ready")
        xn_ready = s.sem("xn_ready")
        turned = s.sem("turned")
        placed = s.sem("placed")
        own_act = s.sem("own_act")
        own = s.sem("own_vector")
        block = s.block()

        def pairs(engine, body):
            with engine.Fori(0, LATENT_TILES // 2) as i:
                body(i, LATENT_COND)
            body(LATENT_TILES // 2, CONTEXT_COND)

        @block.sync
        def _(sp):
            def load(i, _):
                for j in range(2):
                    sp.wait_ge(xn_ready, 2 * i)
                    sp.dma_start(x[:, j, :], io["x"][2 * i + j]).then_inc(x_in[j], 16)
            pairs(sp, load)

        @block.scalar
        def _(act):
            act.wait_ge(eps_ready, 1)

            def body(i, _):
                c = Chain(act, own_act)
                for j in range(2):
                    act.wait_ge(x_in[j], 16 * i + 16)
                    c.link(nc.scalar.activation(square[:, j, :], x[:, j, :], ACT.Square, accum_out=total[:, j:j + 1]))
                    nc.scalar.activation(total[:, j:j + 1], total[:, j:j + 1], ACT.Sqrt, scale=1.0 / D,
                                         bias=eps[:, 0:1]).then_inc(root_ready, 1)
                for j in range(2):
                    act.wait_ge(rstd_ready, 2 * i + j + 1)
                    if j == 0:
                        act.wait_ge(turned, 2 * i)
                    nc.scalar.activation(xn[:, j, :], x[:, j, :], ACT.Copy, scale=rstd[:, j:j + 1])\
                      .then_inc(xn_ready, 1)
                c.reset()
            pairs(act, body)

        @block.tensor
        def _(pe):
            def body(i, _):
                for j in range(2):
                    pe.wait_ge(xn_ready, 2 * i + j + 1)
                    pe.wait_ge(placed, 2 * i)
                    for k in range(KD):
                        last = nc.tensor.transpose(ps[j][:, k, :], xn[:, j, k * P:(k + 1) * P], keep["ident"][:, :])
                    last.then_inc(turned, 1)
            pairs(pe, body)

        @block.vector
        def _(dve):
            nc.vector.memset(eps[:, :], EPS).then_inc(eps_ready, 1)

            def body(i, cnd):
                for j in range(2):
                    dve.wait_ge(root_ready, 2 * i + j + 1)
                    nc.vector.reciprocal(rstd[:, j:j + 1], total[:, j:j + 1]).then_inc(rstd_ready, 1)
                for j in range(2):
                    dve.wait_ge(turned, 2 * i + j + 1)
                    for k in range(KD):
                        last = nc.vector.tensor_scalar(
                            hT[:, k, bass.ts(2 * i + j, P)], ps[j][:, k, :], keep["factor"][:, 0, k, cnd:cnd + 1],
                            keep["mod_cols"][:, 0, k, cnd:cnd + 1], ALU.mult, ALU.add)
                    last.then_inc(placed, 1)
            pairs(dve, body)


RG = dict(conv=0, conv_bias=4, bias_a=5, bias_i=7, lam=9, state=11, decay=13, decay_neg=15)
RG_ROWS, RG_ALL = 13, 17
X0, Y0, Q0, K0 = 1, 5, 9, 13


def projection_and_rg_lru(nc, io, keep, hT, fused, v):
    w_in = io["w_in"].rearrange("(j p) n -> p j n", p=P)
    segments = ((0, LATENT), (LATENT, CONTEXT))
    HALF = SLAB // 2
    SLABS, SLOTS_PER_SLAB = 4, 8
    PRODUCTS = 4 * len(CHUNKS)
    V_UNITS = 2 * TILES
    with Scope(nc, "proj") as s:
        slab = [s.sb(f"slab{n}", [P, KD, HALF]) for n in range(2)]
        k_out = s.sb("k_out", [P, 2, SLAB])
        cols = s.sb("cols", [P, RG_ALL, RG_TILES])
        taps = s.sb("taps", [P, 5])
        now = s.sb("now", [P, RG_ALL])
        work = s.sb("work", [P, 4, 2, RG_TILES])
        weights = s.sb("weights", [P, 4, P])
        states = s.sb("states", [P, 2, RG_TILES])
        r = s.sb("r", [P, T])
        i_gate = s.sb("i_gate", [P, T])
        a_t = s.sb("a_t", [P, T])
        q_t = s.sb("q_t", [P, T])
        h = [s.sb("h_fwd", [P, T]), s.sb("h_bwd", [P, T])]
        ps = [s.psum(f"ps{n}", [P, SLAB]) for n in range(6)]
        gate_ps = [s.psum(f"gate_ps{n}", [P, SLAB]) for n in range(2)]
        slab_in = [s.sem(f"slab_in{n}") for n in range(2)]
        made = s.sem("made")
        taken = s.sem("taken")
        v_made = s.sem("v_made")
        v_taken = s.sem("v_taken")
        k_turned = s.sem("k_turned")
        k_taken = s.sem("k_taken")
        stored = s.sem("stored")
        cols_in = s.sem("cols_in")
        weights_in = s.sem("weights_in")
        e_ready = s.sem("e_ready")
        decay_asked = s.sem("decay_asked")
        now_ready = s.sem("now_ready")
        conv_ready = s.sem("conv_ready")
        product = s.sem("product")
        gates_ready = s.sem("gates_ready")
        decays_ready = s.sem("decays_ready")
        ratio_ready = s.sem("ratio_ready")
        root_ready = s.sem("root_ready")
        scanned = s.sem("scanned")
        gelu_ready = s.sem("gelu_ready")
        tile_done = s.sem("tile_done")
        own_act = s.sem("own_act")
        own = s.sem("own_vector")
        block = s.block()

        def v_units(slot):
            return [u for u in range(V_UNITS) if u * SLOTS_PER_SLAB // V_UNITS == slot]

        @block.sync
        def _(sp):
            def load_half(a, n):
                sp.dma_start(slab[n][:, :, :], w_in[:, :, bass.ds(a * SLAB + n * HALF, HALF)]).then_inc(slab_in[n], 16)

            def load_weights(ct):
                sp.dma_start(weights[:, :, :], io["rg_blocks"][ct]).then_inc(weights_in, 16)

            sp.dma_start(cols[:, 0:RG_ROWS, :], io["rg_cols"]).then_inc(cols_in, 16)
            load_half(0, 0)
            load_half(0, 1)
            load_weights(0)
            sp.wait_ge(made, 2)
            load_half(1, 0)
            sp.wait_ge(made, 4)
            load_half(1, 1)
            with sp.Fori(1, SLABS) as a:
                sp.wait_ge(made, 4 * a + 2)
                load_half(a + 1, 0)
                sp.wait_ge(product, PRODUCTS * a)
                load_weights(a)
                sp.wait_ge(made, 4 * a + 4)
                load_half(a + 1, 1)
            sp.wait_ge(v_taken, V_UNITS)
            sp.wait_ge(k_taken, 2)
            for t in range(2):
                sp.dma_start(io["new_v"][t * P:(t + 1) * P, :], v[:, LATENT_TILES + t, :]).then_inc(stored, 16)
                sp.dma_start(io["new_k"][t * P:(t + 1) * P, :], k_out[:, t, :]).then_inc(stored, 16)
            sp.wait_ge(tile_done, RG_TILES)
            sp.dma_start(io["new_state"], states[:, :, :]).then_inc(stored, 16)
            sp.wait_ge(stored, 80)

        @block.tensor
        def _(pe):
            def gate_products(ct, slot):
                if slot == 0:
                    pe.wait_ge(weights_in, 16 * ct + 16)
                    pe.wait_ge(conv_ready, ct + 1)
                for g in (2 * slot, 2 * slot + 1):
                    if g < PRODUCTS:
                        at, width = CHUNKS[g % 3]
                        pe.wait_ge(gates_ready, PRODUCTS * ct + g + 1)
                        nc.tensor.matmul(gate_ps[g % 2][:, 0:width], weights[:, g // 3, :],
                                         fused[:, ct, at:at + width], start=True, stop=True).then_inc(product, 1)

            def features(a, slot):
                ct, half = slot // 2, slot % 2
                if half == 0:
                    if ct % 2 == 0:
                        pe.wait_ge(slab_in[ct // 2], 16 * a + 16)
                    pe.wait_ge(taken, 4 * a + ct + 1)
                for k in range(half * KD // 2, (half + 1) * KD // 2):
                    for c, (at, width) in enumerate(CHUNKS):
                        last = nc.tensor.matmul(ps[3 * (ct % 2) + c][:, 0:width],
                                                slab[ct // 2][:, k, ct % 2 * P:(ct % 2 + 1) * P],
                                                hT[:, k, at:at + width], start=(k == 0), stop=(k == KD - 1))
                if half == 1:
                    last.then_inc(made, 1)

            for slot in range(SLOTS_PER_SLAB):
                features(0, slot)
            with pe.Fori(1, SLABS) as a:
                for slot in range(SLOTS_PER_SLAB):
                    gate_products(a - 1, slot)
                    features(a, slot)
            for slot in range(SLOTS_PER_SLAB):
                gate_products(RG_TILES - 1, slot)
                for u in v_units(slot):
                    t, half = u % TILES, u // TILES
                    if t == 0:
                        pe.wait_ge(slab_in[half], 16 * (SLABS + 1))
                    if u < 6:
                        pe.wait_ge(taken, 4 * SLABS + 2)
                    else:
                        pe.wait_ge(v_taken, u - 5)
                    for k in range(KD):
                        last = nc.tensor.matmul(ps[u % 6][:, 0:HALF], hT[:, k, t * P:(t + 1) * P], slab[half][:, k, :],
                                                start=(k == 0), stop=(k == KD - 1))
                    last.then_inc(v_made, 1)
            pe.wait_ge(v_taken, V_UNITS)
            for t in range(2):
                for j in range(4):
                    last = nc.tensor.transpose(ps[t][:, j * P:(j + 1) * P],
                                               fused[:, K0 + j, LATENT + t * P:LATENT + (t + 1) * P],
                                               keep["ident"][:, :])
                last.then_inc(k_turned, 1)

        @block.scalar
        def _(act):
            act.sem_inc(taken, 2)
            act.sem_inc(gates_ready, 2)

            def copy_features(a, slot):
                if slot % 2:
                    ct = slot // 2
                    act.wait_ge(made, 4 * a + ct + 1)
                    for c, (at, width) in enumerate(CHUNKS):
                        last = nc.scalar.activation(fused[:, X0 + 4 * a + ct, at:at + width],
                                                    ps[3 * (ct % 2) + c][:, 0:width], ACT.Copy)
                    last.then_inc(taken, 1)

            def copy_v(_, slot):
                for u in v_units(slot):
                    t, half = u % TILES, u // TILES
                    act.wait_ge(v_made, u + 1)
                    nc.scalar.activation(v[:, t, half * HALF:(half + 1) * HALF], ps[u % 6][:, 0:HALF], ACT.Copy)\
                      .then_inc(v_taken, 1)

            def tile(ct, copy):
                c = Chain(act, own_act)
                act.wait_ge(now_ready, ct + 1)

                def sigmoids(slot):
                    for g in (2 * slot, 2 * slot + 1):
                        n, (at, width) = g // 3, CHUNKS[g % 3]
                        d, out, row = n // 2, (r, i_gate)[n % 2], (RG["bias_a"], RG["bias_i"])[n % 2] + n // 2
                        if g == 6:
                            act.wait_ge(ratio_ready, 2 * ct + 1)
                        if g == 9:
                            act.wait_ge(scanned, 2 * ct + 1)
                        act.wait_ge(product, PRODUCTS * ct + g + 1)
                        c.link(nc.scalar.activation(out[:, at:at + width], gate_ps[g % 2][:, 0:width], ACT.Sigmoid,
                                                    bias=now[:, row:row + 1]))
                        act.sem_inc(gates_ready, 1)

                def decays(d):
                    decay, decay_neg = RG["decay"] + d, RG["decay_neg"] + d
                    nc.scalar.activation(a_t[:, :], r[:, :], ACT.Exp, scale=now[:, decay:decay + 1])
                    nc.scalar.activation(q_t[:, :], r[:, :], ACT.Tanh, scale=now[:, decay_neg:decay_neg + 1])\
                      .then_inc(decays_ready, 1)

                def root(d):
                    act.wait_ge(ratio_ready, 2 * ct + d + 1)
                    nc.scalar.activation(q_t[:, :], q_t[:, :], ACT.Sqrt, scale=2.0).then_inc(root_ready, 1)

                a = ct + 1
                sigmoids(0); copy(a, 0)
                sigmoids(1); copy(a, 1)
                sigmoids(2); decays(0); copy(a, 2)
                root(0); sigmoids(3); copy(a, 3)
                sigmoids(4); copy(a, 4)
                sigmoids(5); decays(1); copy(a, 5)
                root(1); copy(a, 6)
                copy(a, 7)
                act.wait_ge(taken, 4 + ct + 1 + 2)
                nc.scalar.activation(fused[:, Y0 + ct, :], fused[:, Y0 + ct, :], ACT.Gelu_apprx_tanh)\
                  .then_inc(gelu_ready, 1)
                c.reset()

            act.wait_ge(decay_asked, 1)
            nc.scalar.activation(work[:, 1, :, :], work[:, 0, :, :], ACT.Exp, scale=-1.0).then_inc(e_ready, 1)
            for slot in range(SLOTS_PER_SLAB):
                copy_features(0, slot)
            with act.Fori(0, RG_TILES - 1) as ct:
                tile(ct, copy_features)
            tile(RG_TILES - 1, copy_v)

        @block.vector
        def _(dve):
            dve.wait_ge(cols_in, 16)
            c = Chain(dve, own)
            lam = cols[:, RG["lam"]:RG["lam"] + 2, :]
            z, acc, z2, tmp = [work[:, n, :, :] for n in range(4)]
            c.link(nc.vector.tensor_scalar_mul(z2, lam, -1.0))
            c.link(nc.vector.tensor_tensor(z, lam, z2, ALU.max))
            dve.sem_inc(decay_asked, 1)
            dve.wait_ge(e_ready, 1)
            c.link(nc.vector.tensor_scalar_add(tmp, acc, 2.0))
            c.link(nc.vector.reciprocal(tmp, tmp))
            c.link(nc.vector.tensor_tensor(z, acc, tmp, ALU.mult))
            c.link(nc.vector.tensor_tensor(z2, z, z, ALU.mult))
            c.link(nc.vector.tensor_scalar(acc, z2, 1.0 / 17, 1.0 / 15, ALU.mult, ALU.add))
            for odd in range(13, 0, -2):
                c.link(nc.vector.tensor_tensor(acc, acc, z2, ALU.mult))
                c.link(nc.vector.tensor_scalar_add(acc, acc, 1.0 / odd))
            c.link(nc.vector.tensor_tensor(acc, acc, z, ALU.mult))
            c.link(nc.vector.tensor_scalar(tmp, lam, 0.0, 8.0, ALU.min, ALU.mult))
            c.link(nc.vector.tensor_scalar_mul(acc, acc, 16.0))
            c.link(nc.vector.tensor_tensor(cols[:, RG["decay"]:RG["decay"] + 2, :], tmp, acc, ALU.subtract))
            c.link(nc.vector.tensor_tensor(cols[:, RG["decay_neg"]:RG["decay_neg"] + 2, :], acc, tmp, ALU.subtract))

            def convolve(c, ct):
                c.link(nc.vector.tensor_copy(taps[:, :], cols[:, 0:5, ct]))
                tap_col = lambda n: taps[:, n:n + 1]
                c.link(nc.vector.tensor_scalar(fused[:, ct, :], fused[:, X0 + ct, :], tap_col(2), tap_col(4),
                                               ALU.mult, ALU.add))
                for tap, shift in ((0, -2), (1, -1), (3, 1)):
                    for at, width in segments:
                        lo, hi = at + max(0, -shift), at + width - max(0, shift)
                        c.step(nc.vector.scalar_tensor_tensor(
                            fused[:, ct, lo:hi], fused[:, X0 + ct, lo + shift:hi + shift], tap_col(tap),
                            fused[:, ct, lo:hi], ALU.mult, ALU.add))
                    c.wait()
                dve.sem_inc(conv_ready, 1)

            dve.wait_ge(taken, 1 + 2)
            convolve(c, 0)
            c.reset()

            def tile(ct, is_last):
                c = Chain(dve, own)
                c.link(nc.vector.tensor_copy(now[:, :], cols[:, :, ct]))
                dve.sem_inc(now_ready, 1)
                for d in range(2):
                    dve.wait_ge(gates_ready, PRODUCTS * ct + 6 * d + 6 + 2)
                    c.step(nc.vector.tensor_tensor(i_gate[:, :], i_gate[:, :], fused[:, ct, :], ALU.mult))
                    dve.wait_ge(decays_ready, 2 * ct + d + 1)
                    c.link(nc.vector.tensor_scalar_add(r[:, :], q_t[:, :], 1.0))
                    c.link(nc.vector.reciprocal(r[:, :], r[:, :]))
                    nc.vector.tensor_tensor(q_t[:, :], q_t[:, :], r[:, :], ALU.mult).then_inc(ratio_ready, 1)
                    dve.wait_ge(root_ready, 2 * ct + d + 1)
                    c.link(nc.vector.tensor_tensor(i_gate[:, :], i_gate[:, :], q_t[:, :], ALU.mult))
                    for (at, width), first in zip(segments, (now[:, RG["state"] + d:RG["state"] + d + 1], 0.0)):
                        cut = slice(at, at + width) if d == 0 else \
                            slice(at + width - 1, at - 1 if at else None, -1)
                        c.step(nc.vector.tensor_tensor_scan(h[d][:, cut], a_t[:, cut], i_gate[:, cut], first,
                                                            ALU.mult, ALU.add))
                    c.wait()
                    dve.sem_inc(scanned, 1)
                    if d == 0 and not is_last:
                        convolve(c, ct + 1)
                edge = (T - 1, LATENT)
                for d in range(2):
                    c.step(nc.vector.tensor_copy(states[:, d, bass.ds(ct, 1)], h[d][:, edge[d]:edge[d] + 1]))
                c.wait()
                c.link(nc.vector.tensor_tensor(h[0][:, :], h[0][:, :], h[1][:, :], ALU.add))
                dve.wait_ge(gelu_ready, ct + 1)
                c.link(nc.vector.tensor_tensor(fused[:, Y0 + ct, :], h[0][:, :], fused[:, Y0 + ct, :], ALU.mult))
                dve.sem_inc(tile_done, 1)
                c.reset()

            with dve.Fori(0, RG_TILES - 1) as ct:
                tile(ct, False)
            tile(RG_TILES - 1, True)
            for t in range(2):
                dve.wait_ge(k_turned, t + 1)
                nc.vector.tensor_copy(k_out[:, t, :], ps[t][:, :]).then_inc(k_taken, 1)
            dve.wait_ge(v_made, V_UNITS)
            nc.vector.tensor_copy(hT[:, 4:8, :], fused[:, Y0:Y0 + 4, :])


def attention(nc, io, keep, fused, v, catT):
    SPAN = 9 * GRID_W
    with Scope(nc, "att") as s:
        bias = fused[:, 0:8, :].rearrange("p a t -> p (a t)")[:, 0:HEADS * ROW_OFFSETS * GRID_W]\
            .rearrange("p (h j c) -> p h j c", h=HEADS, j=ROW_OFFSETS)
        k_ctx = s.sb("k_ctx", [P, 4, PAST])
        v_ctx = s.sb("v_ctx", [P, 2, 512])
        q_own = s.sb("q_own", [P, HEADS, P])
        score = s.sb("score", [P, 2, SPAN + PAST])
        prob = s.sb("prob", [P, 2, SPAN + PAST])
        probT = s.sb("probT", [P, 2, 7, P])
        low = s.sb("low", [P, HEADS])
        total = s.sb("total", [P, HEADS])
        share = s.sb("share", [P, HEADS])
        att = s.sb("att", [P, 512])
        s_ps = [s.psum(f"s_ps{n}", [P, 2 * SLAB]) for n in range(2)]
        t_ps = s.psum("t_ps", [P, 2 * SLAB])
        o_ps = s.psum("o_ps", [P, SLAB])
        a_ps = s.psum("a_ps", [P, SLAB])
        ctx_in = s.sem("ctx_in")
        bias_in = s.sem("bias_in")
        bias_ready = s.sem("bias_ready")
        zeroed = s.sem("zeroed")
        q_ready = s.sem("q_ready")
        s_made = s.sem("s_made")
        s_taken = s.sem("s_taken")
        low_ready = s.sem("low_ready")
        prob_ready = s.sem("prob_ready")
        prob_turned = s.sem("prob_turned")
        probT_ready = s.sem("probT_ready")
        o_made = s.sem("o_made")
        att_ready = s.sem("att_ready")
        att_turned = s.sem("att_turned")
        att_placed = s.sem("att_placed")
        own_pool = s.sem("own_pool")
        own = s.sem("own_vector")
        block = s.block()

        def tiles(engine, body):
            with engine.Fori(0, 2) as n:
                body(n, n, 0, 7 - 2 * n, 8 * GRID_W, 1)
            with engine.Fori(2, 4) as n:
                body(n, n + 4, 8 * GRID_W, 7 - 2 * n, 8 * GRID_W, 1)
            with engine.Fori(4, 8) as n:
                body(n, n - 2, (n - 4) * P, 3, SPAN, 2)
            with engine.Fori(8, 10) as n:
                body(n, n, LATENT, 0, 0, 2)

        def parts(width):
            out = [(at, min(P, width - at)) for at in range(0, width, P)]
            return out + [(width, P), (width + P, P)]

        @block.sync
        def _(sp):
            sp.dma_start(k_ctx[:, :, :], io["k_ctxT"]).then_inc(ctx_in, 16)
            sp.dma_start(v_ctx[:, :, :], io["v_ctx"].rearrange("l p n -> p l n")).then_inc(ctx_in, 16)
            sp.wait_ge(bias_ready, 1)
            for half in range(2):
                sp.dma_start(bias[half * 64:half * 64 + 64, :, half:half + 15, :], io["rel_bias"]).then_inc(bias_in, 16)

        @block.gpsimd
        def _(pool):
            c = Chain(pool, own_pool)
            for half in range(2):
                c.step(nc.gpsimd.memset(bias[half * 64:half * 64 + 64, :, 15 - 15 * half, :], NEG))
            c.wait()
            pool.sem_inc(bias_ready, 1)
            nc.gpsimd.memset(q_own[:, :, :], 0.0).then_inc(zeroed, 1)
            pool.wait_ge(bias_in, 32)
            rows = HEADS * ROW_OFFSETS
            for half in range(2):
                flat = bias[half * 64:half * 64 + 64, :, :, :].rearrange("p h j c -> p (h j) c")
                left, right = flat[:, :, 0:48], flat[:, :, 16:64]
                c.link(nc.gpsimd.affine_select(out=left, in_=left, compare_op=ALU.is_ge, fill=NEG, base=8,
                                               pattern=[[0, rows], [1, 48]], channel_multiplier=-1))
                c.link(nc.gpsimd.affine_select(out=right, in_=right, compare_op=ALU.is_ge, fill=NEG, base=7 - 16,
                                               pattern=[[0, rows], [-1, 48]], channel_multiplier=1))
            pool.sem_inc(bias_ready, 1)
            pool.wait_ge(s_taken, 4 * HEADS)
            c.step(nc.gpsimd.memset(bias[0:64, :, 7 + 4, :], NEG))
            c.step(nc.gpsimd.memset(bias[64:128, :, 7 - 4, :], NEG))
            c.wait()
            pool.sem_inc(bias_ready, 1)

        @block.tensor
        def _(pe):
            pe.wait_ge(ctx_in, 32)

            def body(n, b, key0, _, width, __):
                pe.wait_ge(q_ready, n + 1)
                keys = parts(width)

                def scores(h):
                    pe.wait_ge(s_taken, 8 * n + h - 1) if h >= 2 else pe.wait_ge(s_taken, 8 * n)
                    for at in range(0, width, SLAB):
                        w = min(SLAB, width - at)
                        nc.tensor.matmul(s_ps[h % 2][:, at:at + w], q_own[:, h, :],
                                         fused[:, K0 + h // 2, bass.ds(key0 + at, w)], start=True, stop=True)
                    rhs = k_ctx[:, h // 2, :] if width else fused[:, K0 + h // 2, LATENT:T]
                    nc.tensor.matmul(s_ps[h % 2][:, width:width + PAST], q_own[:, h, :], rhs,
                                     start=True, stop=True).then_inc(s_made, 1)

                def turn(h):
                    pe.wait_ge(prob_ready, 8 * n + h + 1)
                    pe.wait_ge(probT_ready, 8 * n + h)
                    for i, (at, w) in enumerate(keys):
                        last = nc.tensor.transpose(t_ps[0:w, i * P:(i + 1) * P], prob[:, h % 2, at:at + w],
                                                   keep["ident"][:, :])
                    last.then_inc(prob_turned, 1)

                def weigh(h):
                    pe.wait_ge(probT_ready, 8 * n + h + 1)
                    if h == 0:
                        pe.wait_ge(att_ready, n)
                    for i, (at, w) in enumerate(keys):
                        cut = slice(h * HD, (h + 1) * HD)
                        if at < width:
                            rhs = v[0:w, at // P + (key0 // P if isinstance(key0, int) else n - 4), cut]
                        else:
                            rhs = v_ctx[:, (at - width) // P, cut] if width else v[:, LATENT_TILES + at // P, cut]
                        last = nc.tensor.matmul(o_ps[:, cut], probT[0:w, h % 2, i, :], rhs,
                                                start=(i == 0), stop=(i == len(keys) - 1))
                    last.then_inc(o_made, 1)

                scores(0)
                scores(1)
                for h in range(HEADS + 1):
                    if h + 2 < HEADS:
                        scores(h + 2)
                    if h < HEADS:
                        turn(h)
                    if h >= 1:
                        weigh(h - 1)
                pe.wait_ge(att_ready, n + 1)
                pe.wait_ge(att_placed, n)
                for j in range(4):
                    last = nc.tensor.transpose(a_ps[:, j * P:(j + 1) * P], att[:, j * P:(j + 1) * P],
                                               keep["ident"][:, :])
                last.then_inc(att_turned, 1)
            tiles(pe, body)

        @block.scalar
        def _(act):
            def body(n, b, key0, _, width, __):
                full = width + PAST
                keys = parts(width)

                def exp(h):
                    act.wait_ge(low_ready, 8 * n + h + 1)
                    if h >= 2:
                        act.wait_ge(prob_turned, 8 * n + h - 1)
                    nc.scalar.activation(prob[:, h % 2, 0:full], score[:, h % 2, 0:full], ACT.Exp,
                                         bias=low[:, h:h + 1], accum_out=total[:, h:h + 1]).then_inc(prob_ready, 1)

                def move(h):
                    act.wait_ge(prob_turned, 8 * n + h + 1)
                    act.wait_ge(o_made, 8 * n + h - 1) if h >= 2 else act.wait_ge(o_made, 8 * n)
                    whole = [i for i, (_, w) in enumerate(keys) if w == P]
                    for i, (_, w) in enumerate(keys):
                        if w < P:
                            nc.scalar.activation(probT[0:w, h % 2, i, :], t_ps[0:w, i * P:(i + 1) * P], ACT.Copy)
                    for lo, hi in ((0, 4), (5, 7)) if width == SPAN else ((0, min(4, len(keys))), (4, len(keys))):
                        if hi > lo:
                            last = nc.scalar.activation(probT[:, h % 2, lo:hi, :],
                                                        t_ps[:, lo * P:hi * P].rearrange("p (i q) -> p i q", q=P),
                                                        ACT.Copy)
                    last.then_inc(probT_ready, 1)

                for h in range(HEADS + 1):
                    if h < HEADS:
                        exp(h)
                    if h >= 1:
                        move(h - 1)
                act.wait_ge(att_turned, n + 1)
                nc.scalar.activation(catT[:, 0:4, bass.ds(b * P, P)], a_ps[:, :].rearrange("p (j q) -> p j q", q=P),
                                     ACT.Copy).then_inc(att_placed, 1)
            tiles(act, body)

        @block.vector
        def _(dve):
            dve.wait_ge(zeroed, 1)

            def body(n, b, key0, offset, width, generation):
                c = Chain(dve, own)
                dve.wait_ge(s_made, 8 * n)
                for half in range(2):
                    rows = slice(64 * half, 64 * half + 64)
                    c.step(nc.vector.tensor_scalar_mul(q_own[rows, half::2, :], fused[rows, Q0:Q0 + 4, bass.ds(b * P, P)],
                                                       ATT_SCALE))
                c.wait()
                dve.sem_inc(q_ready, 1)
                if width:
                    dve.wait_ge(bias_ready, 1 + generation)
                for h in range(HEADS):
                    dve.wait_ge(s_made, 8 * n + h + 1)
                    dve.wait_ge(prob_ready, 8 * n + h - 1) if h >= 2 else dve.wait_ge(prob_ready, 8 * n)
                    if width:
                        c.step(nc.vector.tensor_tensor(
                            score[:, h % 2, 0:width], s_ps[h % 2][:, 0:width],
                            fused_bias(bias, h, offset, width), ALU.add))
                    c.step(nc.vector.tensor_copy(score[:, h % 2, width:width + PAST],
                                                 s_ps[h % 2][:, width:width + PAST]))
                    c.wait()
                    dve.sem_inc(s_taken, 1)
                    nc.vector.tensor_reduce(low[:, h:h + 1], score[:, h % 2, 0:width + PAST], AX, ALU.max,
                                            negate=True).then_inc(low_ready, 1)
                dve.wait_ge(prob_ready, 8 * n + 8)
                c.link(nc.vector.reciprocal(share[:, :], total[:, :]))
                dve.wait_ge(o_made, 8 * n + 8)
                dve.wait_ge(att_turned, n)
                nc.vector.tensor_tensor(att[:, :].rearrange("p (h d) -> p h d", h=HEADS),
                                        o_ps[:, :].rearrange("p (h d) -> p h d", h=HEADS),
                                        share[:, :].unsqueeze(2).broadcast_to([P, HEADS, HD]),
                                        ALU.mult).then_inc(att_ready, 1)
                c.reset()

            def fused_bias(bias, h, offset, width):
                return bias[:, h, :, :].rearrange("p j c -> p (j c)")[:, bass.ds(offset * GRID_W, width)]
            tiles(dve, body)


def out_projection(nc, io, keep, catT, scratch):
    with Scope(nc, "out") as s:
        w = s.sb("w", [P, KD, D])
        gate = s.sb("gate", [P, 2, D])
        cat = s.sb("cat", [P, 2, KD, P])
        x = s.sb("x", [P, 2, D])
        x1 = s.sb("x1", [P, 2, D])
        xn = s.sb("xn", [P, 2, D])
        square = s.sb("square", [P, 2, D])
        h2 = s.sb("h2", [P, 2, KD, P])
        total = s.sb("total", [P, 2])
        rstd = s.sb("rstd", [P, 2])
        eps = s.sb("eps", [P, 1])
        o_ps = [s.psum(f"o_ps{n}", [P, D]) for n in range(2)]
        t_ps = [s.psum(f"t_ps{n}", [P, KD, P]) for n in range(2)]
        w_in = s.sem("w_in")
        x_in = [s.sem(f"x_in{n}") for n in range(2)]
        x1_out = [s.sem(f"x1_out{n}") for n in range(2)]
        h2_out = [s.sem(f"h2_out{n}") for n in range(2)]
        cat_ready = s.sem("cat_ready")
        eps_ready = s.sem("eps_ready")
        projected = s.sem("projected")
        x1_ready = s.sem("x1_ready")
        root_ready = s.sem("root_ready")
        rstd_ready = s.sem("rstd_ready")
        xn_ready = s.sem("xn_ready")
        turned = s.sem("turned")
        h2_ready = s.sem("h2_ready")
        own_act = s.sem("own_act")
        own = s.sem("own_vector")
        block = s.block()

        def pairs(engine, body):
            with engine.Fori(0, LATENT_TILES // 2) as i:
                body(i, LATENT_COND)
            body(LATENT_TILES // 2, CONTEXT_COND)

        @block.sync
        def _(sp):
            sp.dma_start(w[:, :, :], io["w_out"].rearrange("(j p) n -> p j n", p=P)).then_inc(w_in, 16)
            sp.dma_start(gate[:, :, :], scratch["gate"][0]).then_inc(w_in, 16)

            def body(i, _):
                for j in range(2):
                    sp.wait_ge(x1_ready, 2 * i)
                    sp.dma_start(x[:, j, :], io["x"][2 * i + j]).then_inc(x_in[j], 16)
                for j in range(2):
                    sp.wait_ge(x1_ready, 2 * i + j + 1)
                    sp.dma_start(scratch["x1"][2 * i + j], x1[:, j, :]).then_inc(x1_out[j], 16)
                for j in range(2):
                    sp.wait_ge(h2_ready, 2 * i + j + 1)
                    sp.dma_start(scratch["h2T"][2 * i + j], h2[:, j, :, :]).then_inc(h2_out[j], 16)
            pairs(sp, body)
            for j in range(2):
                sp.wait_ge(x1_out[j], 16 * TILES // 2)
                sp.wait_ge(h2_out[j], 16 * TILES // 2)

        @block.tensor
        def _(pe):
            pe.wait_ge(w_in, 32)

            def project(i):
                for j in range(2):
                    pe.wait_ge(cat_ready, 2 * i + j + 1)
                    pe.wait_ge(x1_ready, 2 * i)
                    for half in range(2):
                        for k in range(KD):
                            last = nc.tensor.matmul(o_ps[j][:, half * SLAB:(half + 1) * SLAB], cat[:, j, k, :],
                                                    w[:, k, half * SLAB:(half + 1) * SLAB],
                                                    start=(k == 0), stop=(k == KD - 1))
                    last.then_inc(projected, 1)

            def body(i, _):
                if not isinstance(i, int):
                    project(i + 1)
                for j in range(2):
                    pe.wait_ge(xn_ready, 2 * i + j + 1)
                    pe.wait_ge(h2_ready, 2 * i)
                    for k in range(KD):
                        last = nc.tensor.transpose(t_ps[j][:, k, :], xn[:, j, k * P:(k + 1) * P], keep["ident"][:, :])
                    last.then_inc(turned, 1)
            project(0)
            pairs(pe, body)

        @block.scalar
        def _(act):
            act.wait_ge(eps_ready, 1)

            def copy(i):
                for j in range(2):
                    act.wait_ge(projected, 2 * i)
                    nc.scalar.activation(cat[:, j, :, :], catT[:, :, bass.ds((2 * i + j) * P, P)], ACT.Copy)\
                      .then_inc(cat_ready, 1)

            copy(0)

            def body(i, _):
                c = Chain(act, own_act)
                if not isinstance(i, int):
                    copy(i + 1)
                for j in range(2):
                    act.wait_ge(x1_ready, 2 * i + j + 1)
                    c.link(nc.scalar.activation(square[:, j, :], x1[:, j, :], ACT.Square, accum_out=total[:, j:j + 1]))
                    nc.scalar.activation(total[:, j:j + 1], total[:, j:j + 1], ACT.Sqrt, scale=1.0 / D,
                                         bias=eps[:, 0:1]).then_inc(root_ready, 1)
                for j in range(2):
                    act.wait_ge(rstd_ready, 2 * i + j + 1)
                    act.wait_ge(turned, 2 * i)
                    nc.scalar.activation(xn[:, j, :], x1[:, j, :], ACT.Copy, scale=rstd[:, j:j + 1])\
                      .then_inc(xn_ready, 1)
                c.reset()
            pairs(act, body)

        @block.vector
        def _(dve):
            nc.vector.memset(eps[:, :], EPS).then_inc(eps_ready, 1)

            def body(i, cnd):
                c = Chain(dve, own)
                for j in range(2):
                    dve.wait_ge(projected, 2 * i + j + 1)
                    dve.wait_ge(x1_out[j], 16 * i)
                    dve.wait_ge(xn_ready, 2 * i)
                    c.link(nc.vector.tensor_tensor(x1[:, j, :], o_ps[j][:, :], gate[:, cnd, :], ALU.mult))
                    dve.wait_ge(x_in[j], 16 * i + 16)
                    nc.vector.tensor_tensor(x1[:, j, :], x1[:, j, :], x[:, j, :], ALU.add).then_inc(x1_ready, 1)
                for j in range(2):
                    dve.wait_ge(root_ready, 2 * i + j + 1)
                    nc.vector.reciprocal(rstd[:, j:j + 1], total[:, j:j + 1]).then_inc(rstd_ready, 1)
                for j in range(2):
                    dve.wait_ge(turned, 2 * i + j + 1)
                    dve.wait_ge(h2_out[j], 16 * i)
                    for k in range(KD):
                        last = nc.vector.tensor_scalar(
                            h2[:, j, k, :], t_ps[j][:, k, :], keep["factor"][:, 1, k, cnd:cnd + 1],
                            keep["mod_cols"][:, 3, k, cnd:cnd + 1], ALU.mult, ALU.add)
                    last.then_inc(h2_ready, 1)
                c.reset()
            pairs(dve, body)


def routing(nc, io, keep, scratch, first, second, weight, expert_id, share):
    SLABS = PEER_HEADS // 2
    UNITS = SLABS * TILES
    with Scope(nc, "route") as s:
        h2T = s.sb("h2T", [P, TILES, KD, P])
        slab = s.sb("slab", [P, 2, KD, SLAB])
        keysT = s.sb("keysT", [P, 2, N_KEYS])
        qT = s.sb("qT", [P, 4, T])
        score = s.sb("score", [P, TILES, SLAB])
        mine = s.sb("mine", [P, 2, 4, N_KEYS])
        rest = s.sb("rest", [P, 2, 4, N_KEYS])
        top = s.sb("top", [P, 2, 4, TOPK])
        top_at = s.sb("top_at", [P, 2, 4, TOPK], U32)
        top_key = s.sb("top_key", [P, 2, 4, TOPK])
        cand = s.sb("cand", [P, 2, 2, TOPK, TOPK])
        cand_rest = s.sb("cand_rest", [P, 2, 2, TOPK, TOPK])
        best = s.sb("best", [P, 2, 2, TOPK])
        best_at = s.sb("best_at", [P, 2, 2, TOPK], U32)
        rank = s.sb("rank", [P, 2, 2, 2, TOPK], U32)
        rank_f = s.sb("rank_f", [P, 2, 4, TOPK])
        hit = s.sb("hit", [P, 2, 4, TOPK, TOPK])
        norm = s.sb("norm", [P, TILES * PEER_HEADS])
        h2 = s.sb("h2", [P, 2, D])
        q_ps = [s.psum(f"q_ps{n}", [P, SLAB]) for n in range(4)]
        s_ps = [s.psum(f"s_ps{n}", [P, SLAB]) for n in range(2)]
        h_ps = s.psum("h_ps", [P, D])
        h2_in = s.sem("h2_in")
        slab_in = [s.sem(f"slab_in{n}") for n in range(2)]
        slab_done = [s.sem(f"slab_done{n}") for n in range(2)]
        q_made = s.sem("q_made")
        q_ready = s.sem("q_ready")
        s_made = s.sem("s_made")
        s_ready = s.sem("s_ready")
        mine_ready = s.sem("mine_ready")
        mine_used = s.sem("mine_used")
        tops_ready = s.sem("tops_ready")
        cand_ready = s.sem("cand_ready")
        hit_asked = s.sem("hit_asked")
        hit_ready = s.sem("hit_ready")
        weight_ready = s.sem("weight_ready")
        e_ready = s.sem("e_ready")
        turned = s.sem("turned")
        h2_ready = s.sem("h2_ready")
        h2_out = [s.sem(f"h2_out{n}") for n in range(2)]
        passed = s.sem("passed")
        searching = s.sem("searching")
        own = s.sem("own_vector")
        block = s.block()

        def chunks():
            for c, (at, width) in enumerate(CHUNKS):
                yield c, at, width, range(at // P, (at + width) // P)

        @block.sync
        def _(sp):
            w_q = io["w_q"].rearrange("(j p) n -> p j n", p=P)
            sp.dma_start(slab[:, 0, :, :], w_q[:, :, 0:SLAB]).then_inc(slab_in[0], 16)
            for c, at, width, tiles in chunks():
                sp.dma_start(h2T[:, tiles[0]:tiles[-1] + 1, :, :],
                             scratch["h2T"][tiles[0]:tiles[-1] + 1].rearrange("t p k n -> p t k n")).then_inc(h2_in, 16)
                if c == 0:
                    sp.dma_start(keysT[:, :, :], io["keysT"]).then_inc(h2_in, 16)
            sp.dma_start(slab[:, 1, :, :], w_q[:, :, SLAB:2 * SLAB]).then_inc(slab_in[1], 16)
            for a in range(2, SLABS):
                sp.wait_ge(slab_done[a % 2], a // 2)
                sp.dma_start(slab[:, a % 2, :, :], w_q[:, :, a * SLAB:(a + 1) * SLAB]).then_inc(slab_in[a % 2], 16)
            for i in range(GATHER_TILES):
                sp.wait_ge(h2_ready, i + 1)
                sp.dma_start(scratch["h2"][i], h2[:, i % 2, :]).then_inc(h2_out[i % 2], 16)
            for n in range(2):
                sp.wait_ge(h2_out[n], 16 * GATHER_TILES // 2)

        @block.tensor
        def _(pe):
            pe.wait_ge(h2_in, 64)
            with pe.Fori(0, SLABS // 2) as a:
                for n in range(2):
                    pe.wait_ge(slab_in[n], 16 * a + 16)
                    for c, at, width, tiles in chunks():
                        for ct in range(4):
                            turn = 12 * n + 4 * c + ct
                            if turn >= 4:
                                pe.wait_ge(q_ready, 24 * a + turn - 3)
                            else:
                                pe.wait_ge(q_ready, 24 * a)
                            for k in range(KD):
                                last = nc.tensor.matmul(q_ps[ct][:, 0:width].rearrange("p (t n) -> p t n", n=P),
                                                        slab[:, n, k, ct * P:(ct + 1) * P],
                                                        h2T[:, tiles[0]:tiles[-1] + 1, k, :],
                                                        start=(k == 0), stop=(k == KD - 1))
                            last.then_inc(q_made, 1)
                        pe.wait_ge(q_ready, 24 * a + 12 * n + 4 * c + 4)
                        for t in tiles:
                            if TILES * n + t >= 2:
                                pe.wait_ge(s_ready, 2 * TILES * a + TILES * n + t - 1)
                            else:
                                pe.wait_ge(s_ready, 2 * TILES * a)
                            for ct in range(4):
                                last = nc.tensor.matmul(s_ps[t % 2][:, ct * P:(ct + 1) * P],
                                                        qT[:, ct, t * P:(t + 1) * P], keysT[:, ct % 2, :],
                                                        start=True, stop=True)
                            last.then_inc(s_made, 1)
                    pe.wait_ge(q_made, 24 * a + 12 * n + 12)
                    pe.sem_inc(slab_done[n], 1)
            for i in range(GATHER_TILES):
                if i:
                    pe.wait_ge(h2_ready, i)
                for k in range(KD):
                    last = nc.tensor.transpose(h_ps[:, k * P:(k + 1) * P], h2T[:, DENSE_TILES + i, k, :],
                                               keep["ident"][:, :])
                last.then_inc(turned, 1)

        @block.scalar
        def _(act):
            with act.Fori(0, SLABS // 2) as a:
                for n in range(2):
                    for c, at, width, tiles in chunks():
                        if n:
                            act.wait_ge(s_made, 2 * TILES * a + tiles[-1] + 1)
                        else:
                            act.wait_ge(s_made, 2 * TILES * a)
                        for ct in range(4):
                            act.wait_ge(q_made, 24 * a + 12 * n + 4 * c + ct + 1)
                            nc.scalar.activation(qT[:, ct, at:at + width], q_ps[ct][:, 0:width], ACT.Copy)\
                              .then_inc(q_ready, 1)
                        for t in tiles:
                            act.wait_ge(s_made, 2 * TILES * a + TILES * n + t + 1)
                            act.wait_ge(mine_ready, 2 * TILES * a + TILES * n + t + 1)
                            nc.scalar.activation(score[:, t, :], s_ps[t % 2][:, :], ACT.Copy).then_inc(s_ready, 1)
            for i in range(GATHER_TILES):
                act.wait_ge(turned, i + 1)
                if i >= 2:
                    act.wait_ge(h2_out[i % 2], 16 * (i // 2))
                nc.scalar.activation(h2[:, i % 2, :], h_ps[:, :], ACT.Copy).then_inc(h2_ready, 1)
            act.wait_ge(weight_ready, 1)
            nc.scalar.activation(weight[:, :, :], weight[:, :, :], ACT.Exp).then_inc(e_ready, 1)

        @block.gpsimd
        def _(pool):
            pool.sem_inc(mine_ready, TILES)
            pool.sem_inc(mine_used, 2)

            def copy_scores(unit, x, t):
                pool.wait_ge(s_ready, unit + 1)
                pool.wait_ge(mine_used, unit + 1)
                pool.sem_inc(passed, 1)
                nc.gpsimd.tensor_copy(mine[:, x, :, :], score[:, t, :].rearrange("p (c n) -> p c n", c=4))\
                  .then_inc(mine_ready, 1)

            def sum_pairs(unit, x):
                pool.wait_ge(tops_ready, unit + 1)
                nc.gpsimd.tensor_tensor(
                    cand[:, x, :, :, :], top[:, x, 0::2, :].unsqueeze(3).broadcast_to([P, 2, TOPK, TOPK]),
                    top[:, x, 1::2, :].unsqueeze(2).broadcast_to([P, 2, TOPK, TOPK]), ALU.add).then_inc(cand_ready, 1)

            def pick(unit, x):
                pool.wait_ge(hit_asked, unit + 1)
                nc.gpsimd.tensor_tensor(
                    hit[:, x, :, :, :], hit[:, x, :, :, :],
                    top_key[:, x, :, :].unsqueeze(2).broadcast_to([P, 4, TOPK, TOPK]), ALU.mult).then_inc(hit_ready, 1)

            def turn(unit, t):
                sum_pairs(unit, 0)
                sum_pairs(unit + 1, 1)
                if t is not None:
                    copy_scores(unit + 2, 0, t)
                    copy_scores(unit + 3, 1, t + 1)
                pick(unit, 0)
                pick(unit + 1, 1)

            copy_scores(0, 0, 0)
            copy_scores(1, 1, 1)
            with pool.Fori(0, SLABS - 1) as a:
                with pool.Fori(0, TILES // 2 - 1) as i:
                    turn(TILES * a + 2 * i, 2 * i + 2)
                turn(TILES * a + TILES - 2, 0)
            with pool.Fori(0, TILES // 2 - 1) as i:
                turn(TILES * (SLABS - 1) + 2 * i, 2 * i + 2)
            turn(UNITS - 2, None)

        @block.vector
        def _(dve):
            def collect(unit, x):
                dve.wait_ge(hit_ready, unit + 1)
                for part, out in enumerate((first, second)):
                    last = nc.vector.tensor_reduce(out[:, unit, :].rearrange("p (h s) -> p h s", h=2),
                                                   hit[:, x, part::2, :, :], AX, ALU.add)
                return last

            def turn(unit, before):
                c = Chain(dve, own)
                marks = [0, 0]

                def phase(x, *steps):
                    if marks[x]:
                        dve.wait_ge(own, marks[x])
                    for step in steps:
                        step(x)
                    marks[x] = c.n

                flat = [y[:, :, :, :, :].rearrange("p x h a b -> p x h (a b)") for y in (cand, cand_rest)]

                def largest(lo, source, halves, out):
                    return lambda x: [c.step(nc.vector.max(out[:, x, i, lo:lo + 8], source[:, x, i, :]))
                                      for i in range(halves)]

                def places(lo, source, halves, out, out_at):
                    return lambda x: [c.step(nc.vector.max_index(out_at[:, x, i, lo:lo + 8], out[:, x, i, lo:lo + 8],
                                                                 source[:, x, i, :])) for i in range(halves)]

                def without(source, halves, out, left):
                    return lambda x: [c.step(nc.vector.match_replace(left[:, x, i, :], out[:, x, i, 0:8],
                                                                     source[:, x, i, :], LOWEST))
                                      for i in range(halves)]

                for x in range(2):
                    dve.wait_ge(mine_ready, unit + x + 1 + TILES)
                    dve.sem_inc(searching, 1)
                    phase(x, largest(0, mine, 4, top))
                for x in range(2):
                    phase(x, places(0, mine, 4, top, top_at), without(mine, 4, top, rest))
                if before is not None:
                    for x in range(2):
                        collect(before + x, x).then_inc(own, 1)
                        c.n += 1
                for x in range(2):
                    phase(x, largest(8, rest, 4, top))
                    dve.sem_inc(mine_used, 1)
                for x in range(2):
                    phase(x, places(8, rest, 4, top, top_at))
                    dve.sem_inc(tops_ready, 1)
                for x in range(2):
                    dve.wait_ge(cand_ready, unit + x + 1)
                    phase(x, lambda x: c.step(nc.vector.tensor_copy(top_key[:, x, :, :], top_at[:, x, :, :])),
                          largest(0, flat[0], 2, best))
                for x in range(2):
                    phase(x, places(0, flat[0], 2, best, best_at), without(flat[0], 2, best, flat[1]))
                for x in range(2):
                    phase(x, largest(8, flat[1], 2, best))
                for x in range(2):
                    phase(x, places(8, flat[1], 2, best, best_at),
                          lambda x: c.step(nc.vector.tensor_tensor(
                              weight[:, unit + x, :].rearrange("p (h s) -> p h s", h=2), best[:, x, :, :],
                              best[:, x, :, 0:1].broadcast_to([P, 2, TOPK]), ALU.subtract)))
                for x in range(2):
                    phase(x, lambda x: c.step(nc.vector.tensor_single_scalar(
                              rank[:, x, :, 0, :], best_at[:, x, :, :], 4, ALU.logical_shift_right)),
                          lambda x: c.step(nc.vector.tensor_single_scalar(
                              rank[:, x, :, 1, :], best_at[:, x, :, :], TOPK - 1, ALU.bitwise_and)))
                for x in range(2):
                    phase(x, lambda x: c.step(nc.vector.tensor_copy(
                        rank_f[:, x, :, :], rank[:, x, :, :, :].rearrange("p h q s -> p (h q) s"))))
                for x in range(2):
                    phase(x, lambda x: c.step(nc.vector.tensor_tensor(
                        hit[:, x, :, :, :], rank_f[:, x, :, :].unsqueeze(3).broadcast_to([P, 4, TOPK, TOPK]),
                        keep["iota"][:, 0:TOPK].unsqueeze(1).unsqueeze(1).broadcast_to([P, 4, TOPK, TOPK]),
                        ALU.is_equal)))
                for x in range(2):
                    dve.wait_ge(own, marks[x])
                    dve.sem_inc(hit_asked, 1)
                c.reset()

            turn(0, None)
            with dve.Fori(1, UNITS // 2) as i:
                turn(2 * i, 2 * i - 2)
            c = Chain(dve, own)
            for x in range(2):
                c.step(collect(UNITS - 2 + x, x))
            c.wait()
            dve.sem_inc(weight_ready, 1)
            dve.wait_ge(e_ready, 1)
            grouped = weight[:, :, :].rearrange("p u (h s) -> p (u h) s", s=TOPK)
            c.link(nc.vector.tensor_reduce(norm[:, :], grouped, AX, ALU.add))
            c.link(nc.vector.reciprocal(norm[:, :], norm[:, :]))
            c.link(nc.vector.tensor_tensor(grouped, grouped,
                                           norm[:, :].unsqueeze(2).broadcast_to([P, TILES * PEER_HEADS, TOPK]),
                                           ALU.mult))
            gathered = [y[:, :, :].rearrange("p (a t) s -> p t a s", t=TILES)[:, DENSE_TILES:TILES, :, :]
                        for y in (first, second, weight)]
            ids, shares = [y[:, :].rearrange("p (t a s) -> p t a s", t=GATHER_TILES, a=SLABS) for y in (expert_id, share)]
            for t in range(GATHER_TILES):
                c.step(nc.vector.scalar_tensor_tensor(ids[:, t, :, :], gathered[0][:, t, :, :], float(N_KEYS),
                                                      gathered[1][:, t, :, :], ALU.mult, ALU.add))
            c.step(nc.vector.tensor_copy(shares, gathered[2]))
            c.wait()


def place_weights(nc, io, keep, scratch, first, second, weight, tiles):
    BATCH, BATCHES = 4, 4
    STEP = BATCH * BATCHES
    with Scope(nc, "place") as s:
        mine = s.sb("mine", [P, 3, P])
        cols = s.sb("cols", [P, 3, P])
        hot = s.sb("hot", [P, BATCHES, 2, BATCH, N_KEYS])
        grid = [s.sb(f"grid{n}", [P, N_KEYS, P]) for n in range(2)]
        turn_ps = s.psum("turn_ps", [P, SLAB])
        ps = [s.psum(f"ps{n}", [P, SLAB]) for n in range(BATCHES)]
        mine_ready = s.sem("mine_ready")
        turned = s.sem("turned")
        hot_ready = s.sem("hot_ready")
        left_ready = s.sem("left_ready")
        made = s.sem("made")
        placed = s.sem("placed")
        stored = [s.sem(f"stored{n}") for n in range(2)]
        own = s.sem("own_vector")
        block = s.block()
        steps = P // STEP
        per_tile = steps * BATCHES

        def walk(engine, start, body, end=None):
            with engine.Fori(0, tiles // 2) as i:
                for j in range(2):
                    if start:
                        start(2 * i + j, j, i)
                    with engine.Fori(0, steps) as m:
                        body(2 * i + j, j, m, (2 * i + j) * steps + m)
                    if end:
                        end(2 * i + j, j, i)

        @block.vector
        def _(dve):
            dve.sem_inc(made, BATCHES)
            dve.sem_inc(placed, BATCHES)

            def start(t, j, i):
                c = Chain(dve, own)
                for n, source in enumerate((first, second, weight)):
                    c.step(nc.vector.tensor_copy(
                        mine[:, n, :].rearrange("p (a s) -> p a s", s=2 * TOPK),
                        source[:, :, :].rearrange("p (a t) s -> p t a s", t=TILES)[:, t, :, :]))
                c.wait()
                dve.sem_inc(mine_ready, 1)
                dve.wait_ge(turned, t + 1)
                c.link(nc.vector.tensor_copy(cols[:, :, :], turn_ps[:, 0:3 * P].rearrange("p (n t) -> p n t", n=3)))
                c.reset()

            def body(t, j, m, before):
                for b in range(BATCHES):
                    at = m * STEP + b * BATCH
                    dve.wait_ge(made, BATCHES * before + b + 1)
                    nc.vector.tensor_tensor(
                        hot[:, b, :, :, :], keep["iota"][:, :].unsqueeze(1).unsqueeze(1).broadcast_to([P, 2, BATCH, N_KEYS]),
                        cols[:, 0:2, bass.ds(at, BATCH)].unsqueeze(3).broadcast_to([P, 2, BATCH, N_KEYS]),
                        ALU.is_equal).then_inc(hot_ready, 1)
            walk(dve, start, body)

        @block.gpsimd
        def _(pool):
            def body(t, j, m, before):
                for b in range(BATCHES):
                    at = m * STEP + b * BATCH
                    pool.wait_ge(hot_ready, BATCHES * before + b + 1)
                    nc.gpsimd.tensor_tensor(
                        hot[:, b, 0, :, :], hot[:, b, 0, :, :],
                        cols[:, 2, bass.ds(at, BATCH)].unsqueeze(2).broadcast_to([P, BATCH, N_KEYS]),
                        ALU.mult).then_inc(left_ready, 1)
            walk(pool, None, body)

        @block.tensor
        def _(pe):
            def start(t, j, i):
                pe.wait_ge(mine_ready, t + 1)
                for n in range(3):
                    last = nc.tensor.transpose(turn_ps[:, n * P:(n + 1) * P], mine[:, n, :], keep["ident"][:, :])
                last.then_inc(turned, 1)

            def body(t, j, m, before):
                for b in range(BATCHES):
                    pe.wait_ge(left_ready, BATCHES * before + b + 1)
                    pe.wait_ge(placed, BATCHES * before + b + 1)
                    for k in range(BATCH):
                        last = nc.tensor.matmul(ps[b][:, k * N_KEYS:(k + 1) * N_KEYS], hot[:, b, 0, k, :],
                                                hot[:, b, 1, k, :], start=True, stop=True)
                    last.then_inc(made, 1)
            walk(pe, start, body)

        @block.scalar
        def _(act):
            def start(t, j, i):
                act.wait_ge(stored[j], 16 * i)

            def body(t, j, m, before):
                for b in range(BATCHES):
                    act.wait_ge(made, BATCHES * before + b + 1 + BATCHES)
                    nc.scalar.activation(grid[j][:, :, bass.ds(m * STEP + b * BATCH, BATCH)],
                                         ps[b][:, :].rearrange("p (t n) -> p n t", t=BATCH), ACT.Copy)\
                      .then_inc(placed, 1)
            walk(act, start, body)

        @block.sync
        def _(sp):
            g = scratch["g"].rearrange("b a t -> a b t")
            with sp.Fori(0, tiles // 2) as i:
                for j in range(2):
                    sp.wait_ge(placed, (2 * i + j + 1) * per_tile + BATCHES)
                    sp.dma_start(g[:, :, bass.ds((2 * i + j) * P, P)], grid[j][:, :, :]).then_inc(stored[j], 16)
            for j in range(2):
                sp.wait_ge(stored[j], 16 * (tiles // 2))


def experts(nc, io, scratch, expert_id, share):
    ROUNDS, PAIR = N_KEYS // 2, 2
    TOK = DENSE_TILES * P
    HALF = TOK // 2
    BATCH, RING = 8, 4
    PER_TILE = SLOTS // BATCH
    with Scope(nc, "exp") as s:
        xT = [s.sb(f"xT_{n}", [P, KD, TOK], FP32R) for n in ("hi", "lo")]
        u = [s.sb(f"u_{n}", [P, 2, KD, P], FP32R) for n in ("hi", "lo")]
        v = [s.sb(f"v_{n}", [P, 2, PAIR, D], FP32R) for n in ("hi", "lo")]
        w = [s.sb(f"w_{n}", [P, 2, PAIR, TOK], FP32R) for n in ("hi", "lo")]
        acc = s.sb("acc", [P, DENSE_TILES, D])
        u_raw = s.sb("u_raw", [P, KD, P])
        v_raw = s.sb("v_raw", [P, D])
        g_raw = s.sb("g_raw", [P, TOK])
        hidden = s.sb("hidden", [P, 2, TOK])
        u_row = s.sb("u_row", [P, RING, D])
        v_row = s.sb("v_row", [P, RING, D])
        x = s.sb("x", [P, D])
        total = s.sb("total", [P, D])
        u_id = s.sb("u_id", [P, 2, BATCH], I32)
        v_id = s.sb("v_id", [P, 2, BATCH], I32)
        dot = s.sb("dot", [P, 2, BATCH])
        gelu = s.sb("gelu", [P, 2, BATCH])
        factor = s.sb("factor", [P, 2, BATCH])
        a_ps = [s.psum(f"a_ps{n}", [P, 2, SLAB]) for n in range(2)]
        o_ps = [s.psum(f"o_ps{n}", [P, 2, SLAB]) for n in range(2)]
        h2_in = s.sem("h2_in")
        x_hi_ready = s.sem("x_hi_ready")
        xT_ready = s.sem("xT_ready")
        zeroed = s.sem("zeroed")
        u_in = s.sem("u_in")
        v_in = s.sem("v_in")
        g_in = s.sem("g_in")
        u_hi_ready = s.sem("u_hi_ready")
        u_ready = s.sem("u_ready")
        v_hi_ready = s.sem("v_hi_ready")
        v_ready = s.sem("v_ready")
        a_made = s.sem("a_made")
        hidden_ready = s.sem("hidden_ready")
        weighted = s.sem("weighted")
        w_hi_ready = s.sem("w_hi_ready")
        w_ready = s.sem("w_ready")
        o_made = s.sem("o_made")
        added = s.sem("added")
        acc_out = s.sem("acc_out")
        x_in = s.sem("x_in")
        u_row_in = [s.sem(f"u_row_in{n}") for n in range(RING)]
        v_row_in = [s.sem(f"v_row_in{n}") for n in range(RING)]
        dots = s.sem("dots")
        summed = s.sem("summed")
        gelu_ready = s.sem("gelu_ready")
        factor_ready = s.sem("factor_ready")
        total_out = s.sem("total_out")
        passed = s.sem("passed")
        own_pool = s.sem("own_pool")
        block = s.block()

        def f32(a):
            return a.bitcast(FP32)

        def by_round(engine, body):
            body(0, 0, 0)
            body(1, 1, 0)
            with engine.Fori(1, ROUNDS // 2) as i:
                body(2 * i, 0, None)
                body(2 * i + 1, 1, None)
            body(ROUNDS, 0, None)

        def by_tile(engine, body):
            body(0, 0, 0)
            body(1, 1, 0)
            with engine.Fori(1, PER_TILE // 2) as i:
                body(2 * i, 0, None)
                body(2 * i + 1, 1, None)
            with engine.Fori(1, GATHER_TILES) as k:
                body(PER_TILE * k, 0, k)
                body(PER_TILE * k + 1, 1, k)
                with engine.Fori(1, PER_TILE // 2) as i:
                    body(PER_TILE * k + 2 * i, 0, None)
                    body(PER_TILE * k + 2 * i + 1, 1, None)
            body(ROUNDS, 0, None)

        def last(r):
            return isinstance(r, int) and r == ROUNDS

        def at_least(r, n):
            return not isinstance(r, int) or r >= n

        @block.sync
        def _(sp):
            sp.dma_start(acc[:, :, :].rearrange("p t (k n) -> p t k n", k=KD),
                         scratch["h2T"][0:DENSE_TILES].rearrange("t p k n -> p t k n")).then_inc(h2_in, 16)

            def load_u(n):
                sp.wait_ge(u_ready, n)
                sp.dma_start(u_raw[:, :, :], io["uT"][n]).then_inc(u_in, 16)

            load_u(0)
            load_u(1)

            def body(r, parity, _):
                if last(r):
                    return
                for e in range(PAIR):
                    n = 2 * r + e
                    sp.wait_ge(v_ready, n)
                    sp.dma_start(v_raw[:, :], io["v_rows"][:, n, :]).then_inc(v_in, 16)
                    sp.wait_ge(weighted, n)
                    sp.dma_start(g_raw[:, :], scratch["g"][n]).then_inc(g_in, 16)
                    load_u(n + 2)
            by_round(sp, body)
            sp.wait_ge(added, DENSE_TILES * (ROUNDS + 1))
            sp.dma_start(scratch["ffn"][0:DENSE_TILES].rearrange("t p n -> p t n"), acc[:, :, :]).then_inc(acc_out, 16)
            sp.wait_ge(acc_out, 16)

        @block.tensor
        def _(pe):
            pe.sem_inc(a_made, 2)
            pe.wait_ge(xT_ready, 1)

            def body(r, parity, _):
                if not last(r):
                    for e in range(PAIR):
                        n = 2 * r + e
                        pe.wait_ge(u_ready, n + 1)
                        pe.wait_ge(hidden_ready, n + 1)
                        for k in range(KD):
                            for part, xp in ((0, 0), (0, 1), (1, 0)):
                                for c in range(2):
                                    mm = nc.tensor.matmul(a_ps[e][:, c, 0:HALF], u[part][:, e, k, :],
                                                          xT[xp][:, k, c * HALF:(c + 1) * HALF],
                                                          start=(k == 0 and part == 0 and xp == 0),
                                                          stop=(k == KD - 1 and part == 1))
                        mm.then_inc(a_made, 1)
                if at_least(r, 1):
                    g = r - 1
                    pe.wait_ge(w_ready, 2 * g + 2 + 2)
                    pe.wait_ge(v_ready, 2 * g + 2)
                    for t in range(DENSE_TILES):
                        pe.wait_ge(added, DENSE_TILES * (g + 1) + t - 1)
                        for e in range(PAIR):
                            for part, xp in ((0, 0), (0, 1), (1, 0)):
                                for c in range(2):
                                    mm = nc.tensor.matmul(
                                        o_ps[t % 2][:, c, :], w[part][:, 1 - parity, e, t * P:(t + 1) * P],
                                        v[xp][:, 1 - parity, e, c * SLAB:(c + 1) * SLAB],
                                        start=(e == 0 and part == 0 and xp == 0), stop=(e == 1 and part == 1))
                        mm.then_inc(o_made, 1)
            by_round(pe, body)

        @block.scalar
        def _(act):
            act.sem_inc(hidden_ready, 2)

            def split_u(n, e):
                act.wait_ge(u_in, 16 * n + 16)
                act.wait_ge(a_made, n - 1 + 2)
                nc.scalar.activation(u[0][:, e, :, :], u_raw[:, :, :], ACT.Copy).then_inc(u_hi_ready, 1)

            split_u(0, 0)
            split_u(1, 1)
            act.wait_ge(h2_in, 16)
            for k in range(KD):
                hi = nc.scalar.activation(xT[0][:, k, :].rearrange("p (t n) -> p t n", n=P),
                                          acc[:, :, k * P:(k + 1) * P], ACT.Copy)
            hi.then_inc(x_hi_ready, 1)

            def body(r, parity, _):
                if last(r):
                    return
                for e in range(PAIR):
                    n = 2 * r + e
                    act.wait_ge(v_in, 16 * n + 16)
                    if at_least(r, 2):
                        act.wait_ge(o_made, DENSE_TILES * (r - 1))
                    nc.scalar.activation(v[0][:, parity, e, :], v_raw[:, :], ACT.Copy).then_inc(v_hi_ready, 1)
                    act.wait_ge(a_made, n + 1 + 2)
                    act.wait_ge(w_ready, n - 1 + 2)
                    nc.scalar.activation(hidden[:, e, :].rearrange("p (c n) -> p c n", c=2), a_ps[e][:, :, 0:HALF],
                                         ACT.Gelu).then_inc(hidden_ready, 1)
                    split_u(n + 2, e)
                    act.wait_ge(weighted, n + 1)
                    nc.scalar.activation(w[0][:, parity, e, :], hidden[:, e, :], ACT.Copy).then_inc(w_hi_ready, 1)
                act.wait_ge(dots, BATCH * (r + 1) + RING)
                nc.scalar.activation(gelu[:, parity, :], dot[:, parity, :], ACT.Gelu).then_inc(gelu_ready, 1)
            by_round(act, body)

        @block.gpsimd
        def _(pool):
            def stand(c):
                pool.sem_inc(passed, 1)

            def split(lo, raw, hi, hi_ready, ready, n):
                pool.wait_ge(hi_ready, n + 1)
                nc.gpsimd.tensor_tensor(lo, raw, f32(hi), ALU.subtract).then_inc(ready, 1)

            def split_u(n, e):
                split(u[1][:, e, :, :], u_raw[:, :, :], u[0][:, e, :, :], u_hi_ready, u_ready, n)

            def split_v(r, parity, e):
                split(v[1][:, parity, e, :], v_raw[:, :], v[0][:, parity, e, :], v_hi_ready, v_ready, 2 * r + e)

            split_u(0, 0)
            split_u(1, 1)

            def body(r, parity, tile):
                c = Chain(pool, own_pool)
                if tile is not None and not last(r) and parity == 0:
                    pool.wait_ge(dots, BATCH * r + RING)
                    stand(c)
                    pool.dma_start(x[:, :], scratch["h2"][tile]).then_inc(x_in, 16)
                if tile is not None and parity == 1 and not isinstance(tile, int):
                    pool.wait_ge(summed, BATCH * (r - 1) + RING)
                    stand(c)
                    pool.dma_start(scratch["ffn"][tile + (DENSE_TILES - 1)], total[:, :]).then_inc(total_out, 16)
                if not last(r):
                    c.step(nc.gpsimd.tensor_copy(u_id[:, parity, :], expert_id[:, bass.ds(BATCH * r, BATCH)]))
                if at_least(r, 1):
                    c.step(nc.gpsimd.tensor_copy(v_id[:, parity, :], expert_id[:, bass.ds(BATCH * (r - 1), BATCH)]))
                c.wait()
                for j in range(BATCH):
                    if not last(r):
                        pool.wait_ge(dots, BATCH * r + j + 1)
                    if at_least(r, 1):
                        pool.wait_ge(summed, BATCH * (r - 1) + j + 1)
                    stand(c)
                    if not last(r):
                        nc.gpsimd.indirect_dma_start(
                            out=u_row[:, j % RING, :], out_offset=None, in_=io["u_rows"],
                            in_offset=bass.IndirectOffsetOnAxis(ap=u_id[:, parity, j:j + 1], axis=0))\
                          .then_inc(u_row_in[j % RING], 16)
                    if at_least(r, 1):
                        nc.gpsimd.indirect_dma_start(
                            out=v_row[:, j % RING, :], out_offset=None, in_=io["v_rows"].rearrange("a b n -> (a b) n"),
                            in_offset=bass.IndirectOffsetOnAxis(ap=v_id[:, parity, j:j + 1], axis=0))\
                          .then_inc(v_row_in[j % RING], 16)
                    if not last(r):
                        if j == 1 and at_least(r, 1):
                            split_u(2 * r + 1, 1)
                        if j == 4:
                            split_v(r, parity, 0)
                        if j == 6:
                            split_u(2 * r + 2, 0)
                        if j == 7:
                            split_v(r, parity, 1)
                c.reset()
            by_tile(pool, body)
            pool.wait_ge(summed, BATCH * ROUNDS + RING)
            pool.dma_start(scratch["ffn"][TILES - 1], total[:, :]).then_inc(total_out, 16)
            pool.wait_ge(total_out, 16 * GATHER_TILES)

        @block.vector
        def _(dve):
            dve.sem_inc(w_ready, 2)
            dve.sem_inc(added, DENSE_TILES)
            dve.sem_inc(dots, RING)
            dve.sem_inc(summed, RING)
            dve.wait_ge(x_hi_ready, 1)
            for k in range(KD):
                lo = nc.vector.tensor_tensor(xT[1][:, k, :].rearrange("p (t n) -> p t n", n=P),
                                             acc[:, :, k * P:(k + 1) * P],
                                             f32(xT[0][:, k, :]).rearrange("p (t n) -> p t n", n=P), ALU.subtract)
            lo.then_inc(xT_ready, 1)
            dve.wait_ge(xT_ready, 1)
            nc.vector.memset(acc[:, :, :], 0.0).then_inc(zeroed, 1)
            dve.wait_ge(zeroed, 1)

            def body(r, parity, tile):
                def dot_product(j):
                    if last(r):
                        return
                    if j == 0 and tile is not None and parity == 0:
                        dve.wait_ge(x_in, 16 * tile + 16)
                    dve.wait_ge(u_row_in[j % RING], 32 * r + 16 * (j // RING) + 16)
                    nc.vector.tensor_tensor_reduce(out=u_row[:, j % RING, :], in0=u_row[:, j % RING, :], in1=x[:, :],
                                                   scale=1.0, scalar=0.0, op0=ALU.mult, op1=ALU.add,
                                                   accum_out=dot[:, parity, j:j + 1]).then_inc(dots, 1)

                def factors():
                    if at_least(r, 1):
                        dve.wait_ge(gelu_ready, r)
                        nc.vector.tensor_tensor(factor[:, 1 - parity, :], gelu[:, 1 - parity, :],
                                                share[:, bass.ds(BATCH * (r - 1), BATCH)], ALU.mult)\
                          .then_inc(factor_ready, 1)
                        dve.wait_ge(factor_ready, r)

                def add_row(j):
                    if not at_least(r, 1):
                        return
                    row, by = v_row[:, j % RING, :], factor[:, 1 - parity, j:j + 1]
                    dve.wait_ge(v_row_in[j % RING], 32 * (r - 1) + 16 * (j // RING) + 16)
                    if j == 0 and parity == 1 and tile is not None:
                        dve.wait_ge(total_out, 16 * tile)
                        dve.wait_ge(summed, BATCH * (r - 1) + RING)
                        nc.vector.tensor_scalar(total[:, :], row, by, None, ALU.mult).then_inc(summed, 1)
                    else:
                        dve.wait_ge(summed, BATCH * (r - 1) + j + RING)
                        nc.vector.scalar_tensor_tensor(total[:, :], row, by, total[:, :], ALU.mult, ALU.add)\
                          .then_inc(summed, 1)

                def weigh(e):
                    if not last(r):
                        n = 2 * r + e
                        dve.wait_ge(g_in, 16 * n + 16)
                        dve.wait_ge(hidden_ready, n + 1 + 2)
                        nc.vector.tensor_tensor(hidden[:, e, :], hidden[:, e, :], g_raw[:, :], ALU.mult)\
                          .then_inc(weighted, 1)

                def split_w(e):
                    if not last(r):
                        dve.wait_ge(w_hi_ready, 2 * r + e + 1)
                        nc.vector.tensor_tensor(w[1][:, parity, e, :], hidden[:, e, :], f32(w[0][:, parity, e, :]),
                                                ALU.subtract).then_inc(w_ready, 1)

                def add_tile(back, t):
                    if at_least(r, back):
                        g = r - back
                        dve.wait_ge(o_made, DENSE_TILES * g + t + 1)
                        dve.wait_ge(added, DENSE_TILES * g + t + 1)
                        nc.vector.tensor_tensor(acc[:, t, :], o_ps[t % 2][:, :, :].rearrange("p c n -> p (c n)"),
                                                acc[:, t, :], ALU.add).then_inc(added, 1)

                D, X = dot_product, add_row
                D(0); factors(); X(0); add_tile(2, DENSE_TILES - 2)
                D(1); X(1); add_tile(2, DENSE_TILES - 1)
                D(2); X(2); D(3)
                weigh(0)
                X(3); D(4)
                split_w(0)
                X(4); D(5)
                weigh(1)
                X(5); add_tile(1, 0)
                split_w(1)
                D(6); add_tile(1, 1); X(6); add_tile(1, 2); D(7); add_tile(1, 3); X(7)
                if last(r):
                    add_tile(1, DENSE_TILES - 2)
                    add_tile(1, DENSE_TILES - 1)
            by_tile(dve, body)


def final_norm(nc, io, scratch):
    with Scope(nc, "last") as s:
        norm_w = s.sb("norm_w", [P, D])
        gate = s.sb("gate", [P, 2, D])
        x1 = s.sb("x1", [P, 2, D])
        f = s.sb("f", [P, 2, D])
        y = s.sb("y", [P, 2, D])
        square = s.sb("square", [P, D])
        total = s.sb("total", [P, 2])
        rstd = s.sb("rstd", [P, 2])
        eps = s.sb("eps", [P, 1])
        w_in = s.sem("w_in")
        x_in = [s.sem(f"x_in{n}") for n in range(2)]
        f_in = [s.sem(f"f_in{n}") for n in range(2)]
        y_out = [s.sem(f"y_out{n}") for n in range(2)]
        x2_ready = s.sem("x2_ready")
        root_ready = s.sem("root_ready")
        y_ready = s.sem("y_ready")
        own_act = s.sem("own_act")
        own = s.sem("own_vector")
        block = s.block()

        def pairs(engine, body):
            with engine.Fori(0, LATENT_TILES // 2) as i:
                body(i, LATENT_COND)
            body(LATENT_TILES // 2, CONTEXT_COND)

        @block.sync
        def _(sp):
            sp.dma_start(norm_w[:, :], io["norm_f"].partition_broadcast(P)).then_inc(w_in, 16)
            sp.dma_start(gate[:, :, :], scratch["gate"][1]).then_inc(w_in, 16)

            def body(i, _):
                for j in range(2):
                    sp.wait_ge(y_ready, 2 * i)
                    sp.dma_start(x1[:, j, :], scratch["x1"][2 * i + j]).then_inc(x_in[j], 16)
                    sp.dma_start(f[:, j, :], scratch["ffn"][2 * i + j]).then_inc(f_in[j], 16)
                for j in range(2):
                    sp.wait_ge(y_ready, 2 * i + j + 1)
                    sp.dma_start(io["y"].rearrange("(t p) n -> t p n", p=P)[2 * i + j], y[:, j, :])\
                      .then_inc(y_out[j], 16)
            pairs(sp, body)
            for j in range(2):
                sp.wait_ge(y_out[j], 16 * TILES // 2)

        @block.scalar
        def _(act):
            act.wait_ge(x2_ready, 1)

            def body(i, _):
                c = Chain(act, own_act)
                for j in range(2):
                    act.wait_ge(x2_ready, 2 * i + j + 2)
                    c.link(nc.scalar.activation(square[:, :], f[:, j, :], ACT.Square, accum_out=total[:, j:j + 1]))
                    nc.scalar.activation(total[:, j:j + 1], total[:, j:j + 1], ACT.Sqrt, scale=1.0 / D,
                                         bias=eps[:, 0:1]).then_inc(root_ready, 1)
                c.reset()
            pairs(act, body)

        @block.vector
        def _(dve):
            nc.vector.memset(eps[:, :], EPS).then_inc(x2_ready, 1)
            dve.wait_ge(w_in, 32)

            def body(i, cnd):
                c = Chain(dve, own)
                for j in range(2):
                    dve.wait_ge(f_in[j], 16 * i + 16)
                    c.link(nc.vector.tensor_tensor(f[:, j, :], f[:, j, :], gate[:, cnd, :], ALU.mult))
                    dve.wait_ge(x_in[j], 16 * i + 16)
                    nc.vector.tensor_tensor(f[:, j, :], f[:, j, :], x1[:, j, :], ALU.add).then_inc(x2_ready, 1)
                for j in range(2):
                    dve.wait_ge(root_ready, 2 * i + j + 1)
                    c.link(nc.vector.reciprocal(rstd[:, j:j + 1], total[:, j:j + 1]))
                    dve.wait_ge(y_out[j], 16 * i)
                    nc.vector.scalar_tensor_tensor(y[:, j, :], f[:, j, :], rstd[:, j:j + 1], norm_w[:, :],
                                                   ALU.mult, ALU.mult).then_inc(y_ready, 1)
                c.reset()
            pairs(dve, body)


def program(nc, io, stop=99):
    scratch = {name: nc.dram_tensor(f"scratch_{name}", shape, FP32).ap() for name, shape in SCRATCH.items()}
    with Scope(nc, "keep") as s:
        keep = {
            "ident": s.sb("ident", [P, P]),
            "iota_int": s.sb("iota_int", [P, P], I32),
            "iota": s.sb("iota", [P, P]),
            "mod_cols": s.sb("mod_cols", [P, 6, KD, 2]),
            "factor": s.sb("factor", [P, 2, KD, 2]),
        }
        constants_and_modulation(nc, io, keep, scratch)
        if stop <= 1: return
        with Scope(nc, "mix") as m:
            catT = m.sb("catT", [P, KD, T])
            with Scope(nc, "heads") as h:
                fused = h.sb("fused", [P, K0 + 4, T])
                v = h.sb("v", [P, TILES, SLAB])
                input_norm(nc, io, keep, catT)
                if stop <= 2: return
                projection_and_rg_lru(nc, io, keep, catT, fused, v)
                if stop <= 4: return
                attention(nc, io, keep, fused, v, catT)
            if stop <= 5: return
            out_projection(nc, io, keep, catT, scratch)
            if stop <= 6: return
        with Scope(nc, "peer") as r:
            expert_id = r.sb("expert_id", [P, GATHER_TILES * SLOTS], I32)
            share = r.sb("share", [P, GATHER_TILES * SLOTS])
            with Scope(nc, "routes") as q:
                first = q.sb("first", [P, TILES * PEER_HEADS // 2, 2 * TOPK])
                second = q.sb("second", [P, TILES * PEER_HEADS // 2, 2 * TOPK])
                weight = q.sb("weight", [P, TILES * PEER_HEADS // 2, 2 * TOPK])
                routing(nc, io, keep, scratch, first, second, weight, expert_id, share)
                if stop <= 7: return
                place_weights(nc, io, keep, scratch, first, second, weight, DENSE_TILES)
                if stop <= 8: return
            experts(nc, io, scratch, expert_id, share)
        if stop <= 9: return
        final_norm(nc, io, scratch)


def kernel(**inputs):
    from concourse import bacc
    from concourse.bass_utils import run_bass_kernel_spmd

    nc = bacc.Bacc("TRN2", target_bir_lowering=False, num_devices=1)
    arrays, io = laid_out(inputs), {}
    for name, a in arrays.items():
        io[name] = nc.dram_tensor(f"in_{name}", a.shape, mybir.dt.from_np(a.dtype), kind="ExternalInput").ap()
    for name, shape in OUTPUTS.items():
        io[name] = nc.dram_tensor(f"out_{name}", shape, FP32, kind="ExternalOutput").ap()
    program(nc, io)
    r = run_bass_kernel_spmd(nc, [{f"in_{k}": a for k, a in arrays.items()}], core_ids=[0]).results[0]
    return (r["out_y"][LATENT:].reshape(1, CONTEXT, D), r["out_y"][:LATENT].reshape(1, LATENT, D),
            r["out_new_k"].reshape(1, 1, CONTEXT, HEADS, HD), r["out_new_v"].reshape(1, 1, CONTEXT, HEADS, HD),
            r["out_new_state"].transpose(1, 2, 0).reshape(1, 1, 2, 512))


OUTPUTS = {"y": (T, D), "new_k": (CONTEXT, 512), "new_v": (CONTEXT, 512), "new_state": (P, 2, RG_TILES)}


SCRATCH = {"x1": (TILES, P, D), "h2T": (TILES, P, KD, P), "g": (N_KEYS, P, DENSE_TILES * P), "h2": (GATHER_TILES, P, D), "gate": (2, P, 2, D), "ffn": (TILES, P, D)}


def laid_out(inputs):
    a = {k: np.asarray(x) for k, x in inputs.items()}

    def columns(rows):
        rows = np.atleast_2d(rows)
        return np.ascontiguousarray(rows.reshape(rows.shape[0], -1, P).transpose(2, 0, 1))

    w_in = a["w_in"][0].reshape(D, 5, 512)
    blocks = np.zeros((RG_TILES, P, 4, P), np.float32)
    for n, w in enumerate((a["rg_w_a"][0, 0], a["rg_w_i"][0, 0], a["rg_w_a"][0, 1], a["rg_w_i"][0, 1])):
        for b in range(8):
            at = 64 * (b % 2)
            blocks[b // 2, at:at + 64, n, at:at + 64] = w[b]
    rpb = np.pad(a["rpb"][0], ((0, 0), (0, 0), (48, 48)))
    q_col = np.arange(GRID_W)[:, None]
    k_col = np.arange(GRID_W)[None, :]
    toeplitz = rpb[:, :, k_col - q_col + GRID_W - 1]
    out = {
        "x": np.concatenate([a["x_sample"][0], a["x_prompt"][0]]).reshape(TILES, P, D),
        "cond": np.ascontiguousarray(columns(np.stack([a["c"][0], a["c_ctx"]])).transpose(0, 2, 1)),
        "w_mod": a["w_mod"][0],
        "b_mod": a["b_mod"][0],
        "b_mod_cols": columns(a["b_mod"][0].reshape(6, D)),
        "norm_cols": columns(np.stack([a["norm_mix_w"][0], a["norm_ffn_w"][0]])),
        "norm_f": a["norm_f_w"],
        "w_in": np.ascontiguousarray(w_in[:, [3, 4, 0, 1, 2]].reshape(D, -1)),
        "rel_bias": np.ascontiguousarray(toeplitz.transpose(2, 0, 1, 3)),
        "k_ctxT": np.ascontiguousarray(a["cache_k"][0, 0].reshape(PAST, 4, P).transpose(2, 1, 0)),
        "v_ctx": a["cache_v"][0, 0].reshape(2, P, 512),
        "rg_blocks": blocks,
        "rg_cols": columns(np.concatenate([a["conv_w"][0], a["conv_b"], a["rg_b_a"][0], a["rg_b_i"][0],
                                           a["rg_lambda"][0], a["state_rglru"][0, 0]])),
        "w_out": a["w_out"][0],
        "w_q": a["peer_w_q"][0],
        "keysT": np.ascontiguousarray(a["peer_sub_keys"][0].transpose(2, 0, 1)),
        "uT": np.concatenate([a["peer_u"][0].reshape(N_KEYS, N_KEYS, KD, P).transpose(1, 3, 2, 0),
                              np.zeros((2, P, KD, P), np.float32)]),
        "u_rows": a["peer_u"][0],
        "v_rows": a["peer_v"][0].reshape(N_KEYS, N_KEYS, D),
    }
    return {k: np.ascontiguousarray(x) for k, x in out.items()}
```

```python
from contextlib import ExitStack

import numpy as np
import concourse.bass as bass
from concourse import mybir

FP32 = mybir.dt.float32
FP32R = mybir.dt.float32r
U32 = mybir.dt.uint32
I32 = mybir.dt.int32
ALU = mybir.AluOpType
ACT = mybir.ActivationFunctionType
AX = mybir.AxisListType.X

P = 128
D = 1024
KD = D // P
LATENT, CONTEXT = 1024, 256
T = LATENT + CONTEXT
TILES = T // P
LATENT_TILES = LATENT // P
DENSE_TILES, GATHER_TILES = 6, 4
CHUNKS = ((0, 512), (512, 512), (1024, 256))
SLAB = 512
HEADS, HD = 8, 64
GRID_W, WIN_H, WIN_W = 64, 8, 16
ROW_OFFSETS = 2 * WIN_H
PAST = 256
NEG = -1e30
LOWEST = -3e38
ATT_SCALE = HD ** -0.5
RG_TILES = 4
N_KEYS = 128
PEER_HEADS = 8
TOPK = 16
SLOTS = PEER_HEADS * TOPK
EPS = 1e-6
LATENT_COND, CONTEXT_COND = 0, 1


class Chain:

    def __init__(self, engine, semaphore):
        self.engine, self.semaphore, self.n = engine, semaphore, 0

    def step(self, instruction):
        instruction.then_inc(self.semaphore, 1)
        self.n += 1

    def wait(self):
        self.engine.wait_ge(self.semaphore, self.n)

    def link(self, instruction):
        self.step(instruction)
        self.wait()

    def reset(self):
        self.engine.sem_clear(self.semaphore)
        self.n = 0


class Scope:

    def __init__(self, nc, stage):
        self.nc, self.stage, self.stack, self.semaphores = nc, stage, ExitStack(), []

    def __enter__(self):
        return self

    def __exit__(self, *error):
        return self.stack.__exit__(*error)

    def sb(self, name, shape, dtype=FP32):
        return self.stack.enter_context(self.nc.sbuf_tensor(f"{self.stage}_{name}", shape, dtype))

    def psum(self, name, shape):
        return self.stack.enter_context(self.nc.psum_tensor(f"{self.stage}_{name}", shape, FP32))

    def sem(self, name):
        semaphore = self.stack.enter_context(self.nc.semaphore(f"{self.stage}_{name}"))
        self.semaphores.append(semaphore)
        return semaphore

    def block(self, clear=False):
        if clear:
            self.stack.callback(self.clear_semaphores)
        return self.stack.enter_context(self.nc.Block())

    def clear_semaphores(self):
        for semaphore in self.semaphores:
            self.nc.sync.sem_clear(semaphore)


def constants_and_modulation(nc, io, keep):
    SLABS = 2 * D // SLAB
    w_mod = io["w_mod"].rearrange("(j p) n -> p j n", p=P)
    with Scope(nc, "mod") as s:
        cond = s.sb("cond", [P, KD, 2])
        iota_int = s.sb("iota_int", [P, P], I32)
        slab = s.sb("slab", [P, SLABS, KD, SLAB])
        rows = s.sb("rows", [2, SLABS, SLAB])
        row_ps = [s.psum(f"row_ps{n}", [2, SLAB]) for n in range(SLABS)]
        col_ps = [s.psum(f"col_ps{n}", [P, SLAB]) for n in range(SLABS)]
        small_in = s.sem("small_in")
        slab_in = [s.sem(f"slab_in{n}") for n in range(SLABS)]
        silu_ready = s.sem("silu_ready")
        ident_ready = s.sem("ident_ready")
        rows_made = s.sem("rows_made")
        rows_ready = s.sem("rows_ready")
        cols_ready = s.sem("cols_ready")
        cols_taken = s.sem("cols_taken")
        own = s.sem("own_vector")
        own_pool = s.sem("own_pool")
        block = s.block(clear=True)

        @block.sync
        def _(sp):
            sp.dma_start(cond[:, :, :], io["cond"]).then_inc(small_in, 16)
            sp.dma_start(keep["b_mod"][:, :, :], io["b_mod_cols"]).then_inc(small_in, 16)
            sp.dma_start(keep["norm_col"][:, :, :], io["norm_cols"]).then_inc(small_in, 16)
            for n in range(SLABS):
                sp.dma_start(slab[:, n, :, :], w_mod[:, :, n * SLAB:(n + 1) * SLAB]).then_inc(slab_in[n], 16)

        @block.gpsimd
        def _(pool):
            c = Chain(pool, own_pool)
            c.link(nc.gpsimd.memset(keep["ident"][:, :], 0.0))
            c.link(nc.gpsimd.affine_select(out=keep["ident"][:, :], in_=keep["ident"][:, :],
                                           compare_op=ALU.not_equal, fill=1.0, base=0,
                                           pattern=[[-1, P]], channel_multiplier=1))
            pool.sem_inc(ident_ready, 1)
            c.link(nc.gpsimd.iota(iota_int[:, :], pattern=[[1, P]], base=0, channel_multiplier=0))
            c.link(nc.gpsimd.tensor_copy(keep["iota"][:, :], iota_int[:, :]))

        @block.scalar
        def _(act):
            act.wait_ge(small_in, 48)
            nc.scalar.activation(keep["silu"][:, :, :], cond[:, :, :], ACT.Silu).then_inc(silu_ready, 1)

        @block.tensor
        def _(pe):
            pe.wait_ge(silu_ready, 1)
            pe.wait_ge(ident_ready, 1)
            for n in range(SLABS):
                pe.wait_ge(slab_in[n], 16)
                for k in range(KD):
                    last = nc.tensor.matmul(row_ps[n][:, :], keep["silu"][:, k, :], slab[:, n, k, :],
                                            start=(k == 0), stop=(k == KD - 1))
                last.then_inc(rows_made, 1)
            for n in range(SLABS):
                pe.wait_ge(rows_ready, n + 1)
                for ct in range(4):
                    last = nc.tensor.transpose(col_ps[n][:, 2 * ct:2 * ct + 2], rows[:, n, ct * P:(ct + 1) * P],
                                               keep["ident"][0:2, 0:2])
                last.then_inc(cols_ready, 1)

        @block.vector
        def _(dve):
            mod = keep["mod_cols"]
            for n in range(SLABS):
                dve.wait_ge(rows_made, n + 1)
                nc.vector.tensor_copy(rows[:, n, :], row_ps[n][:, :]).then_inc(rows_ready, 1)
            for n in range(SLABS):
                dve.wait_ge(cols_ready, n + 1)
                tiles = slice(4 * (n % 2), 4 * (n % 2) + 4)
                nc.vector.tensor_tensor(
                    mod[:, n // 2, tiles, :], col_ps[n][:, 0:8].rearrange("p (c b) -> p c b", b=2),
                    keep["b_mod"][:, n // 2, tiles].unsqueeze(2).broadcast_to([P, 4, 2]), ALU.add)\
                  .then_inc(cols_taken, 1)
            dve.wait_ge(cols_taken, SLABS)
            norm_factor(nc, keep, Chain(dve, own), 0)


def norm_factor(nc, keep, c, g):
    c.link(nc.vector.tensor_scalar_add(keep["factor"][:, g, :, :], keep["mod_cols"][:, 3 * g + 1, :, :], 1.0))
    c.link(nc.vector.tensor_tensor(keep["factor"][:, g, :, :], keep["factor"][:, g, :, :],
                                   keep["norm_col"][:, g, :].unsqueeze(2).broadcast_to([P, KD, 2]), ALU.mult))


def input_norm(nc, io, keep, hT):
    with Scope(nc, "norm") as s:
        x = s.sb("x", [P, 2, D])
        xn = s.sb("xn", [P, 2, D])
        square = s.sb("square", [P, 2, D])
        total = s.sb("total", [P, 2])
        rstd = s.sb("rstd", [P, 2])
        eps = s.sb("eps", [P, 1])
        ps = [s.psum(f"ps{n}", [P, KD, P]) for n in range(2)]
        x_in = [s.sem(f"x_in{n}") for n in range(2)]
        eps_ready = s.sem("eps_ready")
        root_ready = s.sem("root_ready")
        rstd_ready = s.sem("rstd_ready")
        xn_ready = s.sem("xn_ready")
        turned = s.sem("turned")
        placed = s.sem("placed")
        own_act = s.sem("own_act")
        block = s.block(clear=True)

        def pairs(engine, body):
            with engine.Fori(0, LATENT_TILES // 2) as i:
                body(i, LATENT_COND)
            body(LATENT_TILES // 2, CONTEXT_COND)

        @block.sync
        def _(sp):
            def load(i, _):
                for j in range(2):
                    sp.wait_ge(xn_ready, 2 * i)
                    sp.dma_start(x[:, j, :], io["x"][2 * i + j]).then_inc(x_in[j], 16)
            pairs(sp, load)

        @block.scalar
        def _(act):
            act.wait_ge(eps_ready, 1)

            def body(i, _):
                c = Chain(act, own_act)
                for j in range(2):
                    act.wait_ge(x_in[j], 16 * i + 16)
                    c.link(nc.scalar.activation(square[:, j, :], x[:, j, :], ACT.Square, accum_out=total[:, j:j + 1]))
                    nc.scalar.activation(total[:, j:j + 1], total[:, j:j + 1], ACT.Sqrt, scale=1.0 / D,
                                         bias=eps[:, 0:1]).then_inc(root_ready, 1)
                for j in range(2):
                    act.wait_ge(rstd_ready, 2 * i + j + 1)
                    if j == 0:
                        act.wait_ge(turned, 2 * i)
                    nc.scalar.activation(xn[:, j, :], x[:, j, :], ACT.Copy, scale=rstd[:, j:j + 1])\
                      .then_inc(xn_ready, 1)
                c.reset()
            pairs(act, body)

        @block.tensor
        def _(pe):
            def body(i, _):
                for j in range(2):
                    pe.wait_ge(xn_ready, 2 * i + j + 1)
                    pe.wait_ge(placed, 2 * i)
                    for k in range(KD):
                        last = nc.tensor.transpose(ps[j][:, k, :], xn[:, j, k * P:(k + 1) * P], keep["ident"][:, :])
                    last.then_inc(turned, 1)
            pairs(pe, body)

        @block.vector
        def _(dve):
            nc.vector.memset(eps[:, :], EPS).then_inc(eps_ready, 1)

            def body(i, cnd):
                for j in range(2):
                    dve.wait_ge(root_ready, 2 * i + j + 1)
                    nc.vector.reciprocal(rstd[:, j:j + 1], total[:, j:j + 1]).then_inc(rstd_ready, 1)
                for j in range(2):
                    dve.wait_ge(turned, 2 * i + j + 1)
                    for k in range(KD):
                        last = nc.vector.tensor_scalar(
                            hT[:, k, bass.ts(2 * i + j, P)], ps[j][:, k, :], keep["factor"][:, 0, k, cnd:cnd + 1],
                            keep["mod_cols"][:, 0, k, cnd:cnd + 1], ALU.mult, ALU.add)
                    last.then_inc(placed, 1)
            pairs(dve, body)


RG = dict(conv=0, conv_bias=4, bias_a=5, bias_i=7, lam=9, state=11, decay=13, decay_neg=15)
RG_ROWS, RG_ALL = 13, 17
X0, Y0, Q0, K0 = 1, 5, 9, 13


def projection_and_rg_lru(nc, io, keep, hT, fused, v):
    w_in = io["w_in"].rearrange("(j p) n -> p j n", p=P)
    segments = ((0, LATENT), (LATENT, CONTEXT))
    HALF = SLAB // 2
    SLABS, SLOTS_PER_SLAB = 4, 8
    PRODUCTS = 4 * len(CHUNKS)
    V_UNITS = 2 * TILES
    with Scope(nc, "proj") as s:
        slab = [s.sb(f"slab{n}", [P, KD, HALF]) for n in range(2)]
        k_out = s.sb("k_out", [P, 2, SLAB])
        cols = s.sb("cols", [P, RG_ALL, RG_TILES])
        taps = s.sb("taps", [P, 5])
        now = s.sb("now", [P, RG_ALL])
        work = s.sb("work", [P, 4, 2, RG_TILES])
        weights = s.sb("weights", [P, 4, P])
        states = s.sb("states", [P, 2, RG_TILES])
        r = s.sb("r", [P, T])
        i_gate = s.sb("i_gate", [P, T])
        a_t = s.sb("a_t", [P, T])
        q_t = s.sb("q_t", [P, T])
        h = [s.sb("h_fwd", [P, T]), s.sb("h_bwd", [P, T])]
        ps = [s.psum(f"ps{n}", [P, SLAB]) for n in range(6)]
        gate_ps = [s.psum(f"gate_ps{n}", [P, SLAB]) for n in range(2)]
        slab_in = [s.sem(f"slab_in{n}") for n in range(2)]
        made = s.sem("made")
        taken = s.sem("taken")
        v_made = s.sem("v_made")
        v_taken = s.sem("v_taken")
        k_turned = s.sem("k_turned")
        k_taken = s.sem("k_taken")
        stored = s.sem("stored")
        cols_in = s.sem("cols_in")
        weights_in = s.sem("weights_in")
        e_ready = s.sem("e_ready")
        decay_asked = s.sem("decay_asked")
        now_ready = s.sem("now_ready")
        conv_ready = s.sem("conv_ready")
        product = s.sem("product")
        gates_ready = s.sem("gates_ready")
        decays_ready = s.sem("decays_ready")
        ratio_ready = s.sem("ratio_ready")
        root_ready = s.sem("root_ready")
        scanned = s.sem("scanned")
        gelu_ready = s.sem("gelu_ready")
        tile_done = s.sem("tile_done")
        own_act = s.sem("own_act")
        own = s.sem("own_vector")
        block = s.block()

        def v_units(slot):
            return [u for u in range(V_UNITS) if u * SLOTS_PER_SLAB // V_UNITS == slot]

        @block.sync
        def _(sp):
            def load_half(a, n):
                sp.dma_start(slab[n][:, :, :], w_in[:, :, bass.ds(a * SLAB + n * HALF, HALF)]).then_inc(slab_in[n], 16)

            def load_weights(ct):
                sp.dma_start(weights[:, :, :], io["rg_blocks"][ct]).then_inc(weights_in, 16)

            sp.dma_start(cols[:, 0:RG_ROWS, :], io["rg_cols"]).then_inc(cols_in, 16)
            load_half(0, 0)
            load_half(0, 1)
            load_weights(0)
            sp.wait_ge(made, 2)
            load_half(1, 0)
            sp.wait_ge(made, 4)
            load_half(1, 1)
            with sp.Fori(1, SLABS) as a:
                sp.wait_ge(made, 4 * a + 2)
                load_half(a + 1, 0)
                sp.wait_ge(product, PRODUCTS * a)
                load_weights(a)
                sp.wait_ge(made, 4 * a + 4)
                load_half(a + 1, 1)
            sp.wait_ge(v_taken, V_UNITS)
            sp.wait_ge(k_taken, 2)
            for t in range(2):
                sp.dma_start(io["new_v"][t * P:(t + 1) * P, :], v[:, LATENT_TILES + t, :]).then_inc(stored, 16)
                sp.dma_start(io["new_k"][t * P:(t + 1) * P, :], k_out[:, t, :]).then_inc(stored, 16)
            sp.wait_ge(tile_done, RG_TILES)
            sp.dma_start(io["new_state"], states[:, :, :]).then_inc(stored, 16)
            sp.wait_ge(stored, 80)

        @block.tensor
        def _(pe):
            def gate_products(ct, slot):
                if slot == 0:
                    pe.wait_ge(weights_in, 16 * ct + 16)
                    pe.wait_ge(conv_ready, ct + 1)
                for g in (2 * slot, 2 * slot + 1):
                    if g < PRODUCTS:
                        at, width = CHUNKS[g % 3]
                        pe.wait_ge(gates_ready, PRODUCTS * ct + g + 1)
                        nc.tensor.matmul(gate_ps[g % 2][:, 0:width], weights[:, g // 3, :],
                                         fused[:, ct, at:at + width], start=True, stop=True).then_inc(product, 1)

            def features(a, slot):
                ct, half = slot // 2, slot % 2
                if half == 0:
                    if ct % 2 == 0:
                        pe.wait_ge(slab_in[ct // 2], 16 * a + 16)
                    pe.wait_ge(taken, 4 * a + ct + 1)
                for k in range(half * KD // 2, (half + 1) * KD // 2):
                    for c, (at, width) in enumerate(CHUNKS):
                        last = nc.tensor.matmul(ps[3 * (ct % 2) + c][:, 0:width],
                                                slab[ct // 2][:, k, ct % 2 * P:(ct % 2 + 1) * P],
                                                hT[:, k, at:at + width], start=(k == 0), stop=(k == KD - 1))
                if half == 1:
                    last.then_inc(made, 1)

            for slot in range(SLOTS_PER_SLAB):
                features(0, slot)
            with pe.Fori(1, SLABS) as a:
                for slot in range(SLOTS_PER_SLAB):
                    gate_products(a - 1, slot)
                    features(a, slot)
            for slot in range(SLOTS_PER_SLAB):
                gate_products(RG_TILES - 1, slot)
                for u in v_units(slot):
                    t, half = u % TILES, u // TILES
                    if t == 0:
                        pe.wait_ge(slab_in[half], 16 * (SLABS + 1))
                    if u < 6:
                        pe.wait_ge(taken, 4 * SLABS + 2)
                    else:
                        pe.wait_ge(v_taken, u - 5)
                    for k in range(KD):
                        last = nc.tensor.matmul(ps[u % 6][:, 0:HALF], hT[:, k, t * P:(t + 1) * P], slab[half][:, k, :],
                                                start=(k == 0), stop=(k == KD - 1))
                    last.then_inc(v_made, 1)
            pe.wait_ge(v_taken, V_UNITS)
            for t in range(2):
                for j in range(4):
                    last = nc.tensor.transpose(ps[t][:, j * P:(j + 1) * P],
                                               fused[:, K0 + j, LATENT + t * P:LATENT + (t + 1) * P],
                                               keep["ident"][:, :])
                last.then_inc(k_turned, 1)

        @block.scalar
        def _(act):
            act.sem_inc(taken, 2)
            act.sem_inc(gates_ready, 2)

            def copy_features(a, slot):
                if slot % 2:
                    ct = slot // 2
                    act.wait_ge(made, 4 * a + ct + 1)
                    for c, (at, width) in enumerate(CHUNKS):
                        last = nc.scalar.activation(fused[:, X0 + 4 * a + ct, at:at + width],
                                                    ps[3 * (ct % 2) + c][:, 0:width], ACT.Copy)
                    last.then_inc(taken, 1)

            def copy_v(_, slot):
                for u in v_units(slot):
                    t, half = u % TILES, u // TILES
                    act.wait_ge(v_made, u + 1)
                    nc.scalar.activation(v[:, t, half * HALF:(half + 1) * HALF], ps[u % 6][:, 0:HALF], ACT.Copy)\
                      .then_inc(v_taken, 1)

            def tile(ct, copy):
                c = Chain(act, own_act)
                act.wait_ge(now_ready, ct + 1)

                def sigmoids(slot):
                    for g in (2 * slot, 2 * slot + 1):
                        n, (at, width) = g // 3, CHUNKS[g % 3]
                        d, out, row = n // 2, (r, i_gate)[n % 2], (RG["bias_a"], RG["bias_i"])[n % 2] + n // 2
                        if g == 6:
                            act.wait_ge(ratio_ready, 2 * ct + 1)
                        if g == 9:
                            act.wait_ge(scanned, 2 * ct + 1)
                        act.wait_ge(product, PRODUCTS * ct + g + 1)
                        c.link(nc.scalar.activation(out[:, at:at + width], gate_ps[g % 2][:, 0:width], ACT.Sigmoid,
                                                    bias=now[:, row:row + 1]))
                        act.sem_inc(gates_ready, 1)

                def decays(d):
                    decay, decay_neg = RG["decay"] + d, RG["decay_neg"] + d
                    nc.scalar.activation(a_t[:, :], r[:, :], ACT.Exp, scale=now[:, decay:decay + 1])
                    nc.scalar.activation(q_t[:, :], r[:, :], ACT.Tanh, scale=now[:, decay_neg:decay_neg + 1])\
                      .then_inc(decays_ready, 1)

                def root(d):
                    act.wait_ge(ratio_ready, 2 * ct + d + 1)
                    nc.scalar.activation(q_t[:, :], q_t[:, :], ACT.Sqrt, scale=2.0).then_inc(root_ready, 1)

                a = ct + 1
                sigmoids(0); copy(a, 0)
                sigmoids(1); copy(a, 1)
                sigmoids(2); decays(0); copy(a, 2)
                root(0); sigmoids(3); copy(a, 3)
                sigmoids(4); copy(a, 4)
                sigmoids(5); decays(1); copy(a, 5)
                root(1); copy(a, 6)
                copy(a, 7)
                act.wait_ge(taken, 4 + ct + 1 + 2)
                nc.scalar.activation(fused[:, Y0 + ct, :], fused[:, Y0 + ct, :], ACT.Gelu_apprx_tanh)\
                  .then_inc(gelu_ready, 1)
                c.reset()

            act.wait_ge(decay_asked, 1)
            nc.scalar.activation(work[:, 1, :, :], work[:, 0, :, :], ACT.Exp, scale=-1.0).then_inc(e_ready, 1)
            for slot in range(SLOTS_PER_SLAB):
                copy_features(0, slot)
            with act.Fori(0, RG_TILES - 1) as ct:
                tile(ct, copy_features)
            tile(RG_TILES - 1, copy_v)

        @block.vector
        def _(dve):
            dve.wait_ge(cols_in, 16)
            c = Chain(dve, own)
            lam = cols[:, RG["lam"]:RG["lam"] + 2, :]
            z, acc, z2, tmp = [work[:, n, :, :] for n in range(4)]
            c.link(nc.vector.tensor_scalar_mul(z2, lam, -1.0))
            c.link(nc.vector.tensor_tensor(z, lam, z2, ALU.max))
            dve.sem_inc(decay_asked, 1)
            dve.wait_ge(e_ready, 1)
            c.link(nc.vector.tensor_scalar_add(tmp, acc, 2.0))
            c.link(nc.vector.reciprocal(tmp, tmp))
            c.link(nc.vector.tensor_tensor(z, acc, tmp, ALU.mult))
            c.link(nc.vector.tensor_tensor(z2, z, z, ALU.mult))
            c.link(nc.vector.tensor_scalar(acc, z2, 1.0 / 17, 1.0 / 15, ALU.mult, ALU.add))
            for odd in range(13, 0, -2):
                c.link(nc.vector.tensor_tensor(acc, acc, z2, ALU.mult))
                c.link(nc.vector.tensor_scalar_add(acc, acc, 1.0 / odd))
            c.link(nc.vector.tensor_tensor(acc, acc, z, ALU.mult))
            c.link(nc.vector.tensor_scalar(tmp, lam, 0.0, 8.0, ALU.min, ALU.mult))
            c.link(nc.vector.tensor_scalar_mul(acc, acc, 16.0))
            c.link(nc.vector.tensor_tensor(cols[:, RG["decay"]:RG["decay"] + 2, :], tmp, acc, ALU.subtract))
            c.link(nc.vector.tensor_tensor(cols[:, RG["decay_neg"]:RG["decay_neg"] + 2, :], acc, tmp, ALU.subtract))

            def convolve(c, ct):
                c.link(nc.vector.tensor_copy(taps[:, :], cols[:, 0:5, ct]))
                tap_col = lambda n: taps[:, n:n + 1]
                c.link(nc.vector.tensor_scalar(fused[:, ct, :], fused[:, X0 + ct, :], tap_col(2), tap_col(4),
                                               ALU.mult, ALU.add))
                for tap, shift in ((0, -2), (1, -1), (3, 1)):
                    for at, width in segments:
                        lo, hi = at + max(0, -shift), at + width - max(0, shift)
                        c.step(nc.vector.scalar_tensor_tensor(
                            fused[:, ct, lo:hi], fused[:, X0 + ct, lo + shift:hi + shift], tap_col(tap),
                            fused[:, ct, lo:hi], ALU.mult, ALU.add))
                    c.wait()
                dve.sem_inc(conv_ready, 1)

            dve.wait_ge(taken, 1 + 2)
            convolve(c, 0)
            c.reset()

            def tile(ct, is_last):
                c = Chain(dve, own)
                c.link(nc.vector.tensor_copy(now[:, :], cols[:, :, ct]))
                dve.sem_inc(now_ready, 1)
                for d in range(2):
                    dve.wait_ge(gates_ready, PRODUCTS * ct + 6 * d + 6 + 2)
                    c.step(nc.vector.tensor_tensor(i_gate[:, :], i_gate[:, :], fused[:, ct, :], ALU.mult))
                    dve.wait_ge(decays_ready, 2 * ct + d + 1)
                    c.link(nc.vector.tensor_scalar_add(r[:, :], q_t[:, :], 1.0))
                    c.link(nc.vector.reciprocal(r[:, :], r[:, :]))
                    nc.vector.tensor_tensor(q_t[:, :], q_t[:, :], r[:, :], ALU.mult).then_inc(ratio_ready, 1)
                    dve.wait_ge(root_ready, 2 * ct + d + 1)
                    c.link(nc.vector.tensor_tensor(i_gate[:, :], i_gate[:, :], q_t[:, :], ALU.mult))
                    for (at, width), first in zip(segments, (now[:, RG["state"] + d:RG["state"] + d + 1], 0.0)):
                        cut = slice(at, at + width) if d == 0 else \
                            slice(at + width - 1, at - 1 if at else None, -1)
                        c.step(nc.vector.tensor_tensor_scan(h[d][:, cut], a_t[:, cut], i_gate[:, cut], first,
                                                            ALU.mult, ALU.add))
                    c.wait()
                    dve.sem_inc(scanned, 1)
                    if d == 0 and not is_last:
                        convolve(c, ct + 1)
                edge = (T - 1, LATENT)
                for d in range(2):
                    c.step(nc.vector.tensor_copy(states[:, d, bass.ds(ct, 1)], h[d][:, edge[d]:edge[d] + 1]))
                c.wait()
                c.link(nc.vector.tensor_tensor(h[0][:, :], h[0][:, :], h[1][:, :], ALU.add))
                dve.wait_ge(gelu_ready, ct + 1)
                c.link(nc.vector.tensor_tensor(fused[:, Y0 + ct, :], h[0][:, :], fused[:, Y0 + ct, :], ALU.mult))
                dve.sem_inc(tile_done, 1)
                c.reset()

            with dve.Fori(0, RG_TILES - 1) as ct:
                tile(ct, False)
            tile(RG_TILES - 1, True)
            for t in range(2):
                dve.wait_ge(k_turned, t + 1)
                nc.vector.tensor_copy(k_out[:, t, :], ps[t][:, :]).then_inc(k_taken, 1)
            dve.wait_ge(v_made, V_UNITS)
            nc.vector.tensor_copy(hT[:, 4:8, :], fused[:, Y0:Y0 + 4, :])


def attention(nc, io, keep, fused, v, catT):
    SPAN = 9 * GRID_W
    MOD_DONE, MOD_HEAD = 2 * KD, 2
    mod = keep["mod_cols"][:, :, :, :].rearrange("p g k c -> p (g k) c")
    b_mod = keep["b_mod"][:, :, :].rearrange("p g k -> p (g k)")
    with Scope(nc, "att") as s:
        bias = fused[:, 0:8, :].rearrange("p a t -> p (a t)")[:, 0:HEADS * ROW_OFFSETS * GRID_W]\
            .rearrange("p (h j c) -> p h j c", h=HEADS, j=ROW_OFFSETS)
        k_ctx = s.sb("k_ctx", [P, 4, PAST])
        v_ctx = s.sb("v_ctx", [P, 2, 512])
        q_own = s.sb("q_own", [P, HEADS, P])
        score = s.sb("score", [P, 2, SPAN + PAST])
        prob = s.sb("prob", [P, 2, SPAN + PAST])
        probT = s.sb("probT", [P, 2, 7, P])
        low = s.sb("low", [P, HEADS])
        total = s.sb("total", [P, HEADS])
        share = s.sb("share", [P, HEADS])
        att = s.sb("att", [P, 512])
        w_mod = s.sb("w_mod", [P, KD, SLAB])
        mod_row = s.sb("mod_row", [2, SLAB])
        s_ps = [s.psum(f"s_ps{n}", [P, 2 * SLAB]) for n in range(2)]
        t_ps = s.psum("t_ps", [P, 2 * SLAB])
        o_ps = s.psum("o_ps", [P, SLAB])
        a_ps = s.psum("a_ps", [P, SLAB])
        ctx_in = s.sem("ctx_in")
        bias_in = s.sem("bias_in")
        bias_ready = s.sem("bias_ready")
        zeroed = s.sem("zeroed")
        q_ready = s.sem("q_ready")
        s_made = s.sem("s_made")
        s_taken = s.sem("s_taken")
        low_ready = s.sem("low_ready")
        prob_ready = s.sem("prob_ready")
        prob_turned = s.sem("prob_turned")
        probT_ready = s.sem("probT_ready")
        o_made = s.sem("o_made")
        att_ready = s.sem("att_ready")
        att_turned = s.sem("att_turned")
        att_placed = s.sem("att_placed")
        w_mod_in = s.sem("w_mod_in")
        mod_made = s.sem("mod_made")
        mod_row_ready = s.sem("mod_row_ready")
        mod_turned = s.sem("mod_turned")
        passed = s.sem("passed")
        mod_taken = s.sem("mod_taken")
        own_pool = s.sem("own_pool")
        own = s.sem("own_vector")
        block = s.block()

        def tiles(engine, body):
            with engine.Fori(0, 2) as n:
                body(n, n + LATENT_TILES, LATENT, 0, 0, 0)
            with engine.Fori(2, 4) as n:
                body(n, n - 2, 0, 11 - 2 * n, 8 * GRID_W, 1)
            with engine.Fori(4, 6) as n:
                body(n, n + 2, 8 * GRID_W, 11 - 2 * n, 8 * GRID_W, 1)
            with engine.Fori(6, 10) as n:
                body(n, n - 4, (n - 6) * P, 3, SPAN, 2)

        def parts(width):
            out = [(at, min(P, width - at)) for at in range(0, width, P)]
            return out + [(width, P), (width + P, P)]

        @block.sync
        def _(sp):
            sp.dma_start(k_ctx[:, :, :], io["k_ctxT"]).then_inc(ctx_in, 16)
            sp.dma_start(v_ctx[:, :, :], io["v_ctx"].rearrange("l p n -> p l n")).then_inc(ctx_in, 16)
            sp.wait_ge(bias_ready, 1)
            for half in range(2):
                sp.dma_start(bias[half * 64:half * 64 + 64, :, half:half + 15, :], io["rel_bias"]).then_inc(bias_in, 16)
            columns = io["w_mod"].rearrange("(j p) n -> p j n", p=P)
            with sp.Fori(0, LATENT_TILES) as n:
                sp.wait_ge(mod_made, n)
                sp.dma_start(w_mod[:, :, :], columns[:, :, bass.ds(n * SLAB + MOD_DONE * P, SLAB)]).then_inc(w_mod_in, 16)

        @block.gpsimd
        def _(pool):
            c = Chain(pool, own_pool)
            for half in range(2):
                c.step(nc.gpsimd.memset(bias[half * 64:half * 64 + 64, :, 15 - 15 * half, :], NEG))
            c.wait()
            pool.sem_inc(bias_ready, 1)
            nc.gpsimd.memset(q_own[:, :, :], 0.0).then_inc(zeroed, 1)
            pool.wait_ge(bias_in, 32)
            rows = HEADS * ROW_OFFSETS
            for half in range(2):
                flat = bias[half * 64:half * 64 + 64, :, :, :].rearrange("p h j c -> p (h j) c")
                left, right = flat[:, :, 0:48], flat[:, :, 16:64]
                c.link(nc.gpsimd.affine_select(out=left, in_=left, compare_op=ALU.is_ge, fill=NEG, base=8,
                                               pattern=[[0, rows], [1, 48]], channel_multiplier=-1))
                c.link(nc.gpsimd.affine_select(out=right, in_=right, compare_op=ALU.is_ge, fill=NEG, base=7 - 16,
                                               pattern=[[0, rows], [-1, 48]], channel_multiplier=1))
            pool.sem_inc(bias_ready, 1)
            pool.wait_ge(s_taken, 6 * HEADS)
            c.step(nc.gpsimd.memset(bias[0:64, :, 7 + 4, :], NEG))
            c.step(nc.gpsimd.memset(bias[64:128, :, 7 - 4, :], NEG))
            c.wait()
            pool.sem_inc(bias_ready, 1)

        @block.tensor
        def _(pe):
            pe.wait_ge(ctx_in, 32)

            def body(n, b, key0, _, width, __):
                pe.wait_ge(q_ready, n + 1)
                keys = parts(width)

                def scores(h):
                    pe.wait_ge(s_taken, 8 * n + h - 1) if h >= 2 else pe.wait_ge(s_taken, 8 * n)
                    for at in range(0, width, SLAB):
                        w = min(SLAB, width - at)
                        nc.tensor.matmul(s_ps[h % 2][:, at:at + w], q_own[:, h, :],
                                         fused[:, K0 + h // 2, bass.ds(key0 + at, w)], start=True, stop=True)
                    rhs = k_ctx[:, h // 2, :] if width else fused[:, K0 + h // 2, LATENT:T]
                    nc.tensor.matmul(s_ps[h % 2][:, width:width + PAST], q_own[:, h, :], rhs,
                                     start=True, stop=True).then_inc(s_made, 1)

                def turn(h):
                    pe.wait_ge(prob_ready, 8 * n + h + 1)
                    pe.wait_ge(probT_ready, 8 * n + h)
                    for i, (at, w) in enumerate(keys):
                        last = nc.tensor.transpose(t_ps[0:w, i * P:(i + 1) * P], prob[:, h % 2, at:at + w],
                                                   keep["ident"][:, :])
                    last.then_inc(prob_turned, 1)

                def weigh(h):
                    pe.wait_ge(probT_ready, 8 * n + h + 1)
                    if h == 0:
                        pe.wait_ge(att_ready, n)
                    for i, (at, w) in enumerate(keys):
                        cut = slice(h * HD, (h + 1) * HD)
                        if at < width:
                            rhs = v[0:w, at // P + (key0 // P if isinstance(key0, int) else n - 6), cut]
                        else:
                            rhs = v_ctx[:, (at - width) // P, cut] if width else v[:, LATENT_TILES + at // P, cut]
                        last = nc.tensor.matmul(o_ps[:, cut], probT[0:w, h % 2, i, :], rhs,
                                                start=(i == 0), stop=(i == len(keys) - 1))
                    last.then_inc(o_made, 1)

                def modulation():
                    pe.wait_ge(w_mod_in, 16 * n - 16)
                    pe.wait_ge(att_placed, n)
                    for k in range(KD):
                        last = nc.tensor.matmul(a_ps[0:2, :], keep["silu"][:, k, :], w_mod[:, k, :],
                                                start=(k == 0), stop=(k == KD - 1))
                    last.then_inc(mod_made, 1)

                def modulation_columns():
                    pe.wait_ge(mod_row_ready, n - 1)
                    pe.sem_inc(passed, 1)
                    for ct in range(4):
                        last = nc.tensor.transpose(a_ps[:, 2 * ct:2 * ct + 2], mod_row[:, ct * P:(ct + 1) * P],
                                                   keep["ident"][0:2, 0:2])
                    last.then_inc(mod_turned, 1)

                scores(0)
                scores(1)
                for h in range(HEADS + 1):
                    if h + 2 < HEADS:
                        scores(h + 2)
                    if h < HEADS:
                        turn(h)
                    if h >= 1:
                        weigh(h - 1)
                    if width and h == MOD_HEAD:
                        modulation()
                    if width and h == MOD_HEAD + 3:
                        modulation_columns()
                pe.wait_ge(att_ready, n + 1)
                if width:
                    pe.wait_ge(mod_taken, n - 1)
                else:
                    pe.wait_ge(att_placed, n)
                for j in range(4):
                    last = nc.tensor.transpose(a_ps[:, j * P:(j + 1) * P], att[:, j * P:(j + 1) * P],
                                               keep["ident"][:, :])
                last.then_inc(att_turned, 1)
            tiles(pe, body)

        @block.scalar
        def _(act):
            def body(n, b, key0, _, width, __):
                full = width + PAST
                keys = parts(width)

                def exp(h):
                    act.wait_ge(low_ready, 8 * n + h + 1)
                    if h >= 2:
                        act.wait_ge(prob_turned, 8 * n + h - 1)
                    nc.scalar.activation(prob[:, h % 2, 0:full], score[:, h % 2, 0:full], ACT.Exp,
                                         bias=low[:, h:h + 1], accum_out=total[:, h:h + 1]).then_inc(prob_ready, 1)

                def move(h):
                    act.wait_ge(prob_turned, 8 * n + h + 1)
                    act.wait_ge(o_made, 8 * n + h - 1) if h >= 2 else act.wait_ge(o_made, 8 * n)
                    whole = [i for i, (_, w) in enumerate(keys) if w == P]
                    for i, (_, w) in enumerate(keys):
                        if w < P:
                            nc.scalar.activation(probT[0:w, h % 2, i, :], t_ps[0:w, i * P:(i + 1) * P], ACT.Copy)
                    for lo, hi in ((0, 4), (5, 7)) if width == SPAN else ((0, min(4, len(keys))), (4, len(keys))):
                        if hi > lo:
                            last = nc.scalar.activation(probT[:, h % 2, lo:hi, :],
                                                        t_ps[:, lo * P:hi * P].rearrange("p (i q) -> p i q", q=P),
                                                        ACT.Copy)
                    last.then_inc(probT_ready, 1)

                for h in range(HEADS + 1):
                    if h < HEADS:
                        exp(h)
                    if h >= 1:
                        move(h - 1)
                act.wait_ge(att_turned, n + 1)
                nc.scalar.activation(catT[:, 0:4, bass.ds(b * P, P)], a_ps[:, :].rearrange("p (j q) -> p j q", q=P),
                                     ACT.Copy).then_inc(att_placed, 1)
            tiles(act, body)

        @block.vector
        def _(dve):
            dve.wait_ge(zeroed, 1)

            def body(n, b, key0, offset, width, generation):
                c = Chain(dve, own)
                dve.wait_ge(s_made, 8 * n)
                for half in range(2):
                    rows = slice(64 * half, 64 * half + 64)
                    c.step(nc.vector.tensor_scalar_mul(q_own[rows, half::2, :], fused[rows, Q0:Q0 + 4, bass.ds(b * P, P)],
                                                       ATT_SCALE))
                c.wait()
                dve.sem_inc(q_ready, 1)
                if width:
                    dve.wait_ge(bias_ready, 1 + generation)
                for h in range(HEADS):
                    dve.wait_ge(s_made, 8 * n + h + 1)
                    dve.wait_ge(prob_ready, 8 * n + h - 1) if h >= 2 else dve.wait_ge(prob_ready, 8 * n)
                    if width:
                        c.step(nc.vector.tensor_tensor(
                            score[:, h % 2, 0:width], s_ps[h % 2][:, 0:width],
                            fused_bias(bias, h, offset, width), ALU.add))
                    c.step(nc.vector.tensor_copy(score[:, h % 2, width:width + PAST],
                                                 s_ps[h % 2][:, width:width + PAST]))
                    c.wait()
                    dve.sem_inc(s_taken, 1)
                    if width and h == MOD_HEAD + 3:
                        dve.wait_ge(mod_made, n - 1)
                        nc.vector.tensor_copy(mod_row[:, :], a_ps[0:2, :]).then_inc(mod_row_ready, 1)
                    if width and h == HEADS - 1:
                        dve.wait_ge(mod_turned, n - 1)
                        nc.vector.tensor_tensor(
                            mod[:, bass.ds(4 * n + (MOD_DONE - 8), 4), :], a_ps[:, 0:8].rearrange("p (c b) -> p c b", b=2),
                            b_mod[:, bass.ds(4 * n + (MOD_DONE - 8), 4)].unsqueeze(2).broadcast_to([P, 4, 2]),
                            ALU.add).then_inc(mod_taken, 1)
                    nc.vector.tensor_reduce(low[:, h:h + 1], score[:, h % 2, 0:width + PAST], AX, ALU.max,
                                            negate=True).then_inc(low_ready, 1)
                dve.wait_ge(prob_ready, 8 * n + 8)
                c.link(nc.vector.reciprocal(share[:, :], total[:, :]))
                dve.wait_ge(o_made, 8 * n + 8)
                dve.wait_ge(att_turned, n)
                nc.vector.tensor_tensor(att[:, :].rearrange("p (h d) -> p h d", h=HEADS),
                                        o_ps[:, :].rearrange("p (h d) -> p h d", h=HEADS),
                                        share[:, :].unsqueeze(2).broadcast_to([P, HEADS, HD]),
                                        ALU.mult).then_inc(att_ready, 1)
                c.reset()

            def fused_bias(bias, h, offset, width):
                return bias[:, h, :, :].rearrange("p j c -> p (j c)")[:, bass.ds(offset * GRID_W, width)]
            tiles(dve, body)


def out_projection(nc, io, keep, catT, scratch):
    with Scope(nc, "out") as s:
        w = s.sb("w", [P, KD, D])
        gate = [s.sb(f"gate{g}", [P, 2, D]) for g in range(2)]
        diagonal = s.sb("diagonal", [P, 2, KD, P])
        ones = s.sb("ones", [P, P])
        cat = s.sb("cat", [P, 2, KD, P])
        x = s.sb("x", [P, 2, D])
        x1 = s.sb("x1", [P, 2, D])
        xn = s.sb("xn", [P, 2, D])
        square = s.sb("square", [P, 2, D])
        total = s.sb("total", [P, 2])
        rstd = s.sb("rstd", [P, 2])
        eps = s.sb("eps", [P, 1])
        o_ps = [s.psum(f"o_ps{n}", [P, D]) for n in range(2)]
        t_ps = [s.psum(f"t_ps{n}", [P, KD, P]) for n in range(2)]
        w_in = s.sem("w_in")
        x_in = [s.sem(f"x_in{n}") for n in range(2)]
        x1_out = [s.sem(f"x1_out{n}") for n in range(2)]
        h2_out = s.sem("h2_out")
        cat_ready = s.sem("cat_ready")
        eps_ready = s.sem("eps_ready")
        projected = s.sem("projected")
        x1_ready = s.sem("x1_ready")
        root_ready = s.sem("root_ready")
        rstd_ready = s.sem("rstd_ready")
        xn_ready = s.sem("xn_ready")
        turned = s.sem("turned")
        h2_ready = s.sem("h2_ready")
        diagonal_ready = s.sem("diagonal_ready")
        gate_made = s.sem("gate_made")
        gate_ready = s.sem("gate_ready")
        gate_out = s.sem("gate_out")
        own_act = s.sem("own_act")
        own = s.sem("own_vector")
        block = s.block()
        GATES = [(g, cnd) for g in range(2) for cnd in range(2)]

        def pairs(engine, body):
            with engine.Fori(0, LATENT_TILES // 2) as i:
                body(i, LATENT_COND)
            body(LATENT_TILES // 2, CONTEXT_COND)

        @block.gpsimd
        def _(pool):
            pool.wait_ge(gate_ready, len(GATES))
            pool.dma_start(scratch["gate"], gate[1][:, :, :]).then_inc(gate_out, 16)
            pool.wait_ge(gate_out, 16)

        @block.sync
        def _(sp):
            sp.dma_start(w[:, :, :], io["w_out"].rearrange("(j p) n -> p j n", p=P)).then_inc(w_in, 16)

            def load_x(i):
                for j in range(2):
                    sp.wait_ge(x1_ready, 2 * i)
                    sp.dma_start(x[:, j, :], io["x"][2 * i + j]).then_inc(x_in[j], 16)

            load_x(0)

            def body(i, _):
                for j in range(2):
                    sp.wait_ge(x1_ready, 2 * i + j + 1)
                    sp.dma_start(scratch["x1"][2 * i + j], x1[:, j, :]).then_inc(x1_out[j], 16)
                if not isinstance(i, int):
                    load_x(i + 1)
            pairs(sp, body)
            sp.wait_ge(h2_ready, DENSE_TILES)
            sp.dma_start(scratch["h2T"], catT[:, :, 0:DENSE_TILES * P]).then_inc(h2_out, 16)
            sp.wait_ge(h2_out, 16)
            for j in range(2):
                sp.wait_ge(x1_out[j], 16 * TILES // 2)

        @block.tensor
        def _(pe):
            for i in range(len(GATES)):
                if i >= 2:
                    pe.wait_ge(gate_ready, i - 1)
                pe.wait_ge(diagonal_ready, i + 1)
                for k in range(KD):
                    last = nc.tensor.matmul(o_ps[i % 2][:, k * P:(k + 1) * P], ones[:, :], diagonal[:, i % 2, k, :],
                                            start=True, stop=True)
                last.then_inc(gate_made, 1)
            pe.wait_ge(gate_ready, len(GATES))
            pe.wait_ge(w_in, 16)

            def project(i):
                for j in range(2):
                    pe.wait_ge(cat_ready, 2 * i + j + 1)
                    if not isinstance(i, int) or i:
                        pe.wait_ge(x1_ready, 2 * i + j - 1)
                    for half in range(2):
                        for k in range(KD):
                            last = nc.tensor.matmul(o_ps[j][:, half * SLAB:(half + 1) * SLAB], cat[:, j, k, :],
                                                    w[:, k, half * SLAB:(half + 1) * SLAB],
                                                    start=(k == 0), stop=(k == KD - 1))
                    last.then_inc(projected, 1)

            def body(i, _):
                if not isinstance(i, int):
                    project(i + 1)
                for j in range(2):
                    pe.wait_ge(xn_ready, 2 * i + j + 1)
                    pe.wait_ge(h2_ready, 2 * i)
                    for k in range(KD):
                        last = nc.tensor.transpose(t_ps[j][:, k, :], xn[:, j, k * P:(k + 1) * P], keep["ident"][:, :])
                    last.then_inc(turned, 1)
            project(0)
            pairs(pe, body)

        @block.scalar
        def _(act):
            for i, (g, cnd) in enumerate(GATES):
                act.wait_ge(gate_made, i + 1)
                nc.scalar.activation(gate[g][:, cnd, :], o_ps[i % 2][:, :], ACT.Copy).then_inc(gate_ready, 1)
            act.wait_ge(eps_ready, 1)

            def copy(i):
                for j in range(2):
                    if not isinstance(i, int) or i:
                        act.wait_ge(projected, 2 * i + j - 1)
                    nc.scalar.activation(cat[:, j, :, :], catT[:, :, bass.ds((2 * i + j) * P, P)], ACT.Copy)\
                      .then_inc(cat_ready, 1)

            copy(0)

            def body(i, _):
                c = Chain(act, own_act)
                if not isinstance(i, int):
                    copy(i + 1)
                for j in range(2):
                    act.wait_ge(x1_ready, 2 * i + j + 1)
                    c.link(nc.scalar.activation(square[:, j, :], x1[:, j, :], ACT.Square, accum_out=total[:, j:j + 1]))
                    nc.scalar.activation(total[:, j:j + 1], total[:, j:j + 1], ACT.Sqrt, scale=1.0 / D,
                                         bias=eps[:, 0:1]).then_inc(root_ready, 1)
                for j in range(2):
                    act.wait_ge(rstd_ready, 2 * i + j + 1)
                    act.wait_ge(turned, 2 * i)
                    nc.scalar.activation(xn[:, j, :], x1[:, j, :], ACT.Copy, scale=rstd[:, j:j + 1])\
                      .then_inc(xn_ready, 1)
                c.reset()
            pairs(act, body)

        @block.vector
        def _(dve):
            nc.vector.memset(eps[:, :], EPS).then_inc(eps_ready, 1)
            c = Chain(dve, own)
            norm_factor(nc, keep, c, 1)
            c.link(nc.vector.memset(ones[:, :], 1.0))
            for i, (g, cnd) in enumerate(GATES):
                if i >= 2:
                    dve.wait_ge(gate_made, i - 1)
                nc.vector.tensor_tensor(
                    diagonal[:, i % 2, :, :], keep["ident"][:, :].unsqueeze(1).broadcast_to([P, KD, P]),
                    keep["mod_cols"][:, 3 * g + 2, :, cnd:cnd + 1].broadcast_to([P, KD, P]),
                    ALU.mult).then_inc(diagonal_ready, 1)
            dve.wait_ge(gate_ready, len(GATES))

            def residual(c, i, cnd):
                for j in range(2):
                    dve.wait_ge(projected, 2 * i + j + 1)
                    dve.wait_ge(x1_out[j], 16 * i)
                    dve.wait_ge(xn_ready, 2 * i)
                    c.link(nc.vector.tensor_tensor(x1[:, j, :], o_ps[j][:, :], gate[0][:, cnd, :], ALU.mult))
                    dve.wait_ge(x_in[j], 16 * i + 16)
                    nc.vector.tensor_tensor(x1[:, j, :], x1[:, j, :], x[:, j, :], ALU.add).then_inc(x1_ready, 1)

            residual(c, 0, LATENT_COND)
            c.reset()

            def body(i, cnd, cnd_after=None):
                c = Chain(dve, own)
                for j in range(2):
                    dve.wait_ge(root_ready, 2 * i + j + 1)
                    nc.vector.reciprocal(rstd[:, j:j + 1], total[:, j:j + 1]).then_inc(rstd_ready, 1)
                if cnd_after is not None:
                    residual(c, i + 1, cnd_after)
                for j in range(2):
                    dve.wait_ge(turned, 2 * i + j + 1)
                    for k in range(KD):
                        last = nc.vector.tensor_scalar(
                            catT[:, k, bass.ds((2 * i + j) * P, P)], t_ps[j][:, k, :],
                            keep["factor"][:, 1, k, cnd:cnd + 1],
                            keep["mod_cols"][:, 3, k, cnd:cnd + 1], ALU.mult, ALU.add)
                    last.then_inc(h2_ready, 1)
                c.reset()
            with dve.Fori(0, LATENT_TILES // 2 - 1) as i:
                body(i, LATENT_COND, LATENT_COND)
            body(LATENT_TILES // 2 - 1, LATENT_COND, CONTEXT_COND)
            body(LATENT_TILES // 2, CONTEXT_COND)


def routing(nc, io, keep, h2T, scratch, first, second, weight, expert_id, share):
    SLABS = PEER_HEADS // 2
    UNITS = SLABS * TILES
    with Scope(nc, "route") as s:
        slab = s.sb("slab", [P, 2, KD, SLAB])
        keysT = s.sb("keysT", [P, 2, N_KEYS])
        qT = s.sb("qT", [P, 4, T])
        score = s.sb("score", [P, TILES, SLAB])
        mine = s.sb("mine", [P, 2, 4, N_KEYS])
        rest = s.sb("rest", [P, 2, 4, N_KEYS])
        top = s.sb("top", [P, 2, 4, TOPK])
        top_at = s.sb("top_at", [P, 2, 4, TOPK], U32)
        top_key = s.sb("top_key", [P, 2, 4, TOPK])
        cand = s.sb("cand", [P, 2, 2, TOPK, TOPK])
        cand_rest = s.sb("cand_rest", [P, 2, 2, TOPK, TOPK])
        best = s.sb("best", [P, 2, 2, TOPK])
        best_at = s.sb("best_at", [P, 2, 2, TOPK], U32)
        rank = s.sb("rank", [P, 2, 2, 2, TOPK], U32)
        rank_f = s.sb("rank_f", [P, 2, 4, TOPK])
        hit = s.sb("hit", [P, 2, 4, TOPK, TOPK])
        norm = s.sb("norm", [P, TILES * PEER_HEADS])
        h2 = s.sb("h2", [P, 2, D])
        q_ps = [s.psum(f"q_ps{n}", [P, SLAB]) for n in range(4)]
        s_ps = [s.psum(f"s_ps{n}", [P, SLAB]) for n in range(2)]
        h_ps = s.psum("h_ps", [P, D])
        keys_in = s.sem("keys_in")
        slab_in = [s.sem(f"slab_in{n}") for n in range(2)]
        slab_done = [s.sem(f"slab_done{n}") for n in range(2)]
        q_made = s.sem("q_made")
        q_ready = s.sem("q_ready")
        s_made = s.sem("s_made")
        s_ready = s.sem("s_ready")
        mine_ready = s.sem("mine_ready")
        mine_used = s.sem("mine_used")
        tops_ready = s.sem("tops_ready")
        cand_ready = s.sem("cand_ready")
        hit_asked = s.sem("hit_asked")
        hit_ready = s.sem("hit_ready")
        weight_ready = s.sem("weight_ready")
        e_ready = s.sem("e_ready")
        turned = s.sem("turned")
        h2_ready = s.sem("h2_ready")
        h2_out = [s.sem(f"h2_out{n}") for n in range(2)]
        passed = s.sem("passed")
        searching = s.sem("searching")
        own = s.sem("own_vector")
        block = s.block()

        def chunks():
            for c, (at, width) in enumerate(CHUNKS):
                yield c, at, width, range(at // P, (at + width) // P)

        @block.sync
        def _(sp):
            w_q = io["w_q"].rearrange("(j p) n -> p j n", p=P)
            sp.dma_start(slab[:, 0, :, :], w_q[:, :, 0:SLAB]).then_inc(slab_in[0], 16)
            sp.dma_start(keysT[:, :, :], io["keysT"]).then_inc(keys_in, 16)
            sp.dma_start(slab[:, 1, :, :], w_q[:, :, SLAB:2 * SLAB]).then_inc(slab_in[1], 16)
            for a in range(2, SLABS):
                sp.wait_ge(slab_done[a % 2], a // 2)
                sp.dma_start(slab[:, a % 2, :, :], w_q[:, :, a * SLAB:(a + 1) * SLAB]).then_inc(slab_in[a % 2], 16)
            for i in range(GATHER_TILES):
                sp.wait_ge(h2_ready, i + 1)
                sp.dma_start(scratch["h2"][i], h2[:, i % 2, :]).then_inc(h2_out[i % 2], 16)
            for n in range(2):
                sp.wait_ge(h2_out[n], 16 * GATHER_TILES // 2)

        @block.tensor
        def _(pe):
            pe.wait_ge(keys_in, 16)
            with pe.Fori(0, SLABS // 2) as a:
                for n in range(2):
                    pe.wait_ge(slab_in[n], 16 * a + 16)
                    for c, at, width, tiles in chunks():
                        for ct in range(4):
                            turn = 12 * n + 4 * c + ct
                            if turn >= 4:
                                pe.wait_ge(q_ready, 24 * a + turn - 3)
                            else:
                                pe.wait_ge(q_ready, 24 * a)
                            for k in range(KD):
                                last = nc.tensor.matmul(q_ps[ct][:, 0:width], slab[:, n, k, ct * P:(ct + 1) * P],
                                                        h2T[:, k, at:at + width],
                                                        start=(k == 0), stop=(k == KD - 1))
                            last.then_inc(q_made, 1)
                        pe.wait_ge(q_ready, 24 * a + 12 * n + 4 * c + 4)
                        for t in tiles:
                            if TILES * n + t >= 2:
                                pe.wait_ge(s_ready, 2 * TILES * a + TILES * n + t - 1)
                            else:
                                pe.wait_ge(s_ready, 2 * TILES * a)
                            for ct in range(4):
                                last = nc.tensor.matmul(s_ps[t % 2][:, ct * P:(ct + 1) * P],
                                                        qT[:, ct, t * P:(t + 1) * P], keysT[:, ct % 2, :],
                                                        start=True, stop=True)
                            last.then_inc(s_made, 1)
                    pe.wait_ge(q_made, 24 * a + 12 * n + 12)
                    pe.sem_inc(slab_done[n], 1)
            for i in range(GATHER_TILES):
                if i:
                    pe.wait_ge(h2_ready, i)
                for k in range(KD):
                    at = (DENSE_TILES + i) * P
                    last = nc.tensor.transpose(h_ps[:, k * P:(k + 1) * P], h2T[:, k, at:at + P],
                                               keep["ident"][:, :])
                last.then_inc(turned, 1)

        @block.scalar
        def _(act):
            with act.Fori(0, SLABS // 2) as a:
                for n in range(2):
                    for c, at, width, tiles in chunks():
                        if n:
                            act.wait_ge(s_made, 2 * TILES * a + tiles[-1] + 1)
                        else:
                            act.wait_ge(s_made, 2 * TILES * a)
                        for ct in range(4):
                            act.wait_ge(q_made, 24 * a + 12 * n + 4 * c + ct + 1)
                            nc.scalar.activation(qT[:, ct, at:at + width], q_ps[ct][:, 0:width], ACT.Copy)\
                              .then_inc(q_ready, 1)
                        for t in tiles:
                            act.wait_ge(s_made, 2 * TILES * a + TILES * n + t + 1)
                            act.wait_ge(mine_ready, 2 * TILES * a + TILES * n + t + 1)
                            nc.scalar.activation(score[:, t, :], s_ps[t % 2][:, :], ACT.Copy).then_inc(s_ready, 1)
            for i in range(GATHER_TILES):
                act.wait_ge(turned, i + 1)
                if i >= 2:
                    act.wait_ge(h2_out[i % 2], 16 * (i // 2))
                nc.scalar.activation(h2[:, i % 2, :], h_ps[:, :], ACT.Copy).then_inc(h2_ready, 1)
            act.wait_ge(weight_ready, 1)
            nc.scalar.activation(weight[:, :, :], weight[:, :, :], ACT.Exp).then_inc(e_ready, 1)

        @block.gpsimd
        def _(pool):
            pool.sem_inc(mine_ready, TILES)
            pool.sem_inc(mine_used, 2)

            def copy_scores(unit, x, t):
                pool.wait_ge(s_ready, unit + 1)
                pool.wait_ge(mine_used, unit + 1)
                pool.sem_inc(passed, 1)
                nc.gpsimd.tensor_copy(mine[:, x, :, :], score[:, t, :].rearrange("p (c n) -> p c n", c=4))\
                  .then_inc(mine_ready, 1)

            def sum_pairs(unit, x):
                pool.wait_ge(tops_ready, unit + 1)
                nc.gpsimd.tensor_tensor(
                    cand[:, x, :, :, :], top[:, x, 0::2, :].unsqueeze(3).broadcast_to([P, 2, TOPK, TOPK]),
                    top[:, x, 1::2, :].unsqueeze(2).broadcast_to([P, 2, TOPK, TOPK]), ALU.add).then_inc(cand_ready, 1)

            def pick(unit, x):
                pool.wait_ge(hit_asked, unit + 1)
                nc.gpsimd.tensor_tensor(
                    hit[:, x, :, :, :], hit[:, x, :, :, :],
                    top_key[:, x, :, :].unsqueeze(2).broadcast_to([P, 4, TOPK, TOPK]), ALU.mult).then_inc(hit_ready, 1)

            def turn(unit, t):
                sum_pairs(unit, 0)
                sum_pairs(unit + 1, 1)
                if t is not None:
                    copy_scores(unit + 2, 0, t)
                    copy_scores(unit + 3, 1, t + 1)
                pick(unit, 0)
                pick(unit + 1, 1)

            copy_scores(0, 0, 0)
            copy_scores(1, 1, 1)
            with pool.Fori(0, SLABS - 1) as a:
                with pool.Fori(0, TILES // 2 - 1) as i:
                    turn(TILES * a + 2 * i, 2 * i + 2)
                turn(TILES * a + TILES - 2, 0)
            with pool.Fori(0, TILES // 2 - 1) as i:
                turn(TILES * (SLABS - 1) + 2 * i, 2 * i + 2)
            turn(UNITS - 2, None)

        @block.vector
        def _(dve):
            def collect(unit, x):
                dve.wait_ge(hit_ready, unit + 1)
                for part, out in enumerate((first, second)):
                    last = nc.vector.tensor_reduce(out[:, unit, :].rearrange("p (h s) -> p h s", h=2),
                                                   hit[:, x, part::2, :, :], AX, ALU.add)
                return last

            def turn(unit, before):
                c = Chain(dve, own)
                marks = [0, 0]

                def phase(x, *steps):
                    if marks[x]:
                        dve.wait_ge(own, marks[x])
                    for step in steps:
                        step(x)
                    marks[x] = c.n

                flat = [y[:, :, :, :, :].rearrange("p x h a b -> p x h (a b)") for y in (cand, cand_rest)]

                def largest(lo, source, halves, out):
                    return lambda x: [c.step(nc.vector.max(out[:, x, i, lo:lo + 8], source[:, x, i, :]))
                                      for i in range(halves)]

                def places(lo, source, halves, out, out_at):
                    return lambda x: [c.step(nc.vector.max_index(out_at[:, x, i, lo:lo + 8], out[:, x, i, lo:lo + 8],
                                                                 source[:, x, i, :])) for i in range(halves)]

                def without(source, halves, out, left):
                    return lambda x: [c.step(nc.vector.match_replace(left[:, x, i, :], out[:, x, i, 0:8],
                                                                     source[:, x, i, :], LOWEST))
                                      for i in range(halves)]

                for x in range(2):
                    dve.wait_ge(mine_ready, unit + x + 1 + TILES)
                    dve.sem_inc(searching, 1)
                    phase(x, largest(0, mine, 4, top))
                for x in range(2):
                    phase(x, places(0, mine, 4, top, top_at), without(mine, 4, top, rest))
                if before is not None:
                    for x in range(2):
                        collect(before + x, x).then_inc(own, 1)
                        c.n += 1
                for x in range(2):
                    phase(x, largest(8, rest, 4, top))
                    dve.sem_inc(mine_used, 1)
                for x in range(2):
                    phase(x, places(8, rest, 4, top, top_at))
                    dve.sem_inc(tops_ready, 1)
                for x in range(2):
                    dve.wait_ge(cand_ready, unit + x + 1)
                    phase(x, lambda x: c.step(nc.vector.tensor_copy(top_key[:, x, :, :], top_at[:, x, :, :])),
                          largest(0, flat[0], 2, best))
                for x in range(2):
                    phase(x, places(0, flat[0], 2, best, best_at), without(flat[0], 2, best, flat[1]))
                for x in range(2):
                    phase(x, largest(8, flat[1], 2, best))
                for x in range(2):
                    phase(x, places(8, flat[1], 2, best, best_at),
                          lambda x: c.step(nc.vector.tensor_tensor(
                              weight[:, unit + x, :].rearrange("p (h s) -> p h s", h=2), best[:, x, :, :],
                              best[:, x, :, 0:1].broadcast_to([P, 2, TOPK]), ALU.subtract)))
                for x in range(2):
                    phase(x, lambda x: c.step(nc.vector.tensor_single_scalar(
                              rank[:, x, :, 0, :], best_at[:, x, :, :], 4, ALU.logical_shift_right)),
                          lambda x: c.step(nc.vector.tensor_single_scalar(
                              rank[:, x, :, 1, :], best_at[:, x, :, :], TOPK - 1, ALU.bitwise_and)))
                for x in range(2):
                    phase(x, lambda x: c.step(nc.vector.tensor_copy(
                        rank_f[:, x, :, :], rank[:, x, :, :, :].rearrange("p h q s -> p (h q) s"))))
                for x in range(2):
                    phase(x, lambda x: c.step(nc.vector.tensor_tensor(
                        hit[:, x, :, :, :], rank_f[:, x, :, :].unsqueeze(3).broadcast_to([P, 4, TOPK, TOPK]),
                        keep["iota"][:, 0:TOPK].unsqueeze(1).unsqueeze(1).broadcast_to([P, 4, TOPK, TOPK]),
                        ALU.is_equal)))
                for x in range(2):
                    dve.wait_ge(own, marks[x])
                    dve.sem_inc(hit_asked, 1)
                c.reset()

            turn(0, None)
            with dve.Fori(1, UNITS // 2) as i:
                turn(2 * i, 2 * i - 2)
            c = Chain(dve, own)
            for x in range(2):
                c.step(collect(UNITS - 2 + x, x))
            c.wait()
            dve.sem_inc(weight_ready, 1)
            dve.wait_ge(e_ready, 1)
            grouped = weight[:, :, :].rearrange("p u (h s) -> p (u h) s", s=TOPK)
            c.link(nc.vector.tensor_reduce(norm[:, :], grouped, AX, ALU.add))
            c.link(nc.vector.reciprocal(norm[:, :], norm[:, :]))
            c.link(nc.vector.tensor_tensor(grouped, grouped,
                                           norm[:, :].unsqueeze(2).broadcast_to([P, TILES * PEER_HEADS, TOPK]),
                                           ALU.mult))
            gathered = [y[:, :, :].rearrange("p (a t) s -> p t a s", t=TILES)[:, DENSE_TILES:TILES, :, :]
                        for y in (first, second, weight)]
            ids, shares = [y[:, :].rearrange("p (t a s) -> p t a s", t=GATHER_TILES, a=SLABS) for y in (expert_id, share)]
            for t in range(GATHER_TILES):
                c.step(nc.vector.scalar_tensor_tensor(ids[:, t, :, :], gathered[0][:, t, :, :], float(N_KEYS),
                                                      gathered[1][:, t, :, :], ALU.mult, ALU.add))
            c.step(nc.vector.tensor_copy(shares, gathered[2]))
            c.wait()


def place_weights(nc, io, keep, scratch, first, second, weight, tiles):
    BATCH, BATCHES = 4, 4
    STEP = BATCH * BATCHES
    with Scope(nc, "place") as s:
        mine = s.sb("mine", [P, 3, P])
        cols = s.sb("cols", [P, 3, P])
        hot = s.sb("hot", [P, BATCHES, 2, BATCH, N_KEYS])
        grid = [s.sb(f"grid{n}", [P, N_KEYS, P]) for n in range(2)]
        turn_ps = s.psum("turn_ps", [P, SLAB])
        ps = [s.psum(f"ps{n}", [P, SLAB]) for n in range(BATCHES)]
        mine_ready = s.sem("mine_ready")
        turned = s.sem("turned")
        hot_ready = s.sem("hot_ready")
        left_ready = s.sem("left_ready")
        made = s.sem("made")
        placed = s.sem("placed")
        stored = [s.sem(f"stored{n}") for n in range(2)]
        own = s.sem("own_vector")
        block = s.block()
        steps = P // STEP
        per_tile = steps * BATCHES

        def walk(engine, start, body):
            with engine.Fori(0, tiles // 2) as i:
                for j in range(2):
                    if start:
                        start(2 * i + j, j, i)
                    with engine.Fori(0, steps) as m:
                        body(2 * i + j, j, m, (2 * i + j) * steps + m)

        @block.vector
        def _(dve):
            dve.sem_inc(made, BATCHES)
            dve.sem_inc(placed, BATCHES)

            def start(t, j, i):
                c = Chain(dve, own)
                for n, source in enumerate((first, second, weight)):
                    c.step(nc.vector.tensor_copy(
                        mine[:, n, :].rearrange("p (a s) -> p a s", s=2 * TOPK),
                        source[:, :, :].rearrange("p (a t) s -> p t a s", t=TILES)[:, t, :, :]))
                c.wait()
                dve.sem_inc(mine_ready, 1)
                dve.wait_ge(turned, t + 1)
                c.link(nc.vector.tensor_copy(cols[:, :, :], turn_ps[:, 0:3 * P].rearrange("p (n t) -> p n t", n=3)))
                c.reset()

            def body(t, j, m, before):
                for b in range(BATCHES):
                    at = m * STEP + b * BATCH
                    dve.wait_ge(made, BATCHES * before + b + 1)
                    nc.vector.tensor_tensor(
                        hot[:, b, :, :, :], keep["iota"][:, :].unsqueeze(1).unsqueeze(1).broadcast_to([P, 2, BATCH, N_KEYS]),
                        cols[:, 0:2, bass.ds(at, BATCH)].unsqueeze(3).broadcast_to([P, 2, BATCH, N_KEYS]),
                        ALU.is_equal).then_inc(hot_ready, 1)
            walk(dve, start, body)

        @block.gpsimd
        def _(pool):
            def body(t, j, m, before):
                for b in range(BATCHES):
                    at = m * STEP + b * BATCH
                    pool.wait_ge(hot_ready, BATCHES * before + b + 1)
                    nc.gpsimd.tensor_tensor(
                        hot[:, b, 0, :, :], hot[:, b, 0, :, :],
                        cols[:, 2, bass.ds(at, BATCH)].unsqueeze(2).broadcast_to([P, BATCH, N_KEYS]),
                        ALU.mult).then_inc(left_ready, 1)
            walk(pool, None, body)

        @block.tensor
        def _(pe):
            def start(t, j, i):
                pe.wait_ge(mine_ready, t + 1)
                for n in range(3):
                    last = nc.tensor.transpose(turn_ps[:, n * P:(n + 1) * P], mine[:, n, :], keep["ident"][:, :])
                last.then_inc(turned, 1)

            def body(t, j, m, before):
                for b in range(BATCHES):
                    pe.wait_ge(left_ready, BATCHES * before + b + 1)
                    pe.wait_ge(placed, BATCHES * before + b + 1)
                    for k in range(BATCH):
                        last = nc.tensor.matmul(ps[b][:, k * N_KEYS:(k + 1) * N_KEYS], hot[:, b, 0, k, :],
                                                hot[:, b, 1, k, :], start=True, stop=True)
                    last.then_inc(made, 1)
            walk(pe, start, body)

        @block.scalar
        def _(act):
            def start(t, j, i):
                act.wait_ge(stored[j], 16 * i)

            def body(t, j, m, before):
                for b in range(BATCHES):
                    act.wait_ge(made, BATCHES * before + b + 1 + BATCHES)
                    nc.scalar.activation(grid[j][:, :, bass.ds(m * STEP + b * BATCH, BATCH)],
                                         ps[b][:, :].rearrange("p (t n) -> p n t", t=BATCH), ACT.Copy)\
                      .then_inc(placed, 1)
            walk(act, start, body)

        @block.sync
        def _(sp):
            g = scratch["g"].rearrange("b a t -> a b t")
            with sp.Fori(0, tiles // 2) as i:
                for j in range(2):
                    sp.wait_ge(placed, (2 * i + j + 1) * per_tile + BATCHES)
                    sp.dma_start(g[:, :, bass.ds((2 * i + j) * P, P)], grid[j][:, :, :]).then_inc(stored[j], 16)
            for j in range(2):
                sp.wait_ge(stored[j], 16 * (tiles // 2))


def experts(nc, io, scratch, expert_id, share):
    ROUNDS, PAIR = N_KEYS // 2, 2
    TOK = DENSE_TILES * P
    HALF = TOK // 2
    BATCH, RING = 8, 4
    PER_TILE = SLOTS // BATCH
    with Scope(nc, "exp") as s:
        xT = [s.sb(f"xT_{n}", [P, KD, TOK], FP32R) for n in ("hi", "lo")]
        u = [s.sb(f"u_{n}", [P, 2, KD, P], FP32R) for n in ("hi", "lo")]
        v = [s.sb(f"v_{n}", [P, 2, PAIR, D], FP32R) for n in ("hi", "lo")]
        w = [s.sb(f"w_{n}", [P, 2, PAIR, TOK], FP32R) for n in ("hi", "lo")]
        acc = s.sb("acc", [P, DENSE_TILES, D])
        h2T = acc[:, :, :].rearrange("p t n -> p (t n)").rearrange("p (k n) -> p k n", k=KD)
        u_raw = s.sb("u_raw", [P, KD, P])
        v_raw = s.sb("v_raw", [P, D])
        g_raw = s.sb("g_raw", [P, TOK])
        hidden = s.sb("hidden", [P, 2, TOK])
        u_row = s.sb("u_row", [P, RING, D])
        v_row = s.sb("v_row", [P, RING, D])
        x = s.sb("x", [P, D])
        total = s.sb("total", [P, D])
        u_id = s.sb("u_id", [P, 2, BATCH], I32)
        v_id = s.sb("v_id", [P, 2, BATCH], I32)
        dot = s.sb("dot", [P, 2, BATCH])
        gelu = s.sb("gelu", [P, 2, BATCH])
        factor = s.sb("factor", [P, 2, BATCH])
        a_ps = [s.psum(f"a_ps{n}", [P, 2, SLAB]) for n in range(2)]
        o_ps = [s.psum(f"o_ps{n}", [P, 2, SLAB]) for n in range(2)]
        h2_in = s.sem("h2_in")
        x_hi_ready = s.sem("x_hi_ready")
        xT_ready = s.sem("xT_ready")
        zeroed = s.sem("zeroed")
        u_in = s.sem("u_in")
        v_in = s.sem("v_in")
        g_in = s.sem("g_in")
        u_hi_ready = s.sem("u_hi_ready")
        u_ready = s.sem("u_ready")
        v_hi_ready = s.sem("v_hi_ready")
        v_ready = s.sem("v_ready")
        a_made = s.sem("a_made")
        hidden_ready = s.sem("hidden_ready")
        weighted = s.sem("weighted")
        w_hi_ready = s.sem("w_hi_ready")
        w_ready = s.sem("w_ready")
        o_made = s.sem("o_made")
        added = s.sem("added")
        acc_out = s.sem("acc_out")
        x_in = s.sem("x_in")
        u_row_in = [s.sem(f"u_row_in{n}") for n in range(RING)]
        v_row_in = [s.sem(f"v_row_in{n}") for n in range(RING)]
        dots = s.sem("dots")
        summed = s.sem("summed")
        gelu_ready = s.sem("gelu_ready")
        factor_ready = s.sem("factor_ready")
        total_out = s.sem("total_out")
        passed = s.sem("passed")
        own_pool = s.sem("own_pool")
        block = s.block()

        def f32(a):
            return a.bitcast(FP32)

        def by_round(engine, body):
            body(0, 0, 0)
            body(1, 1, 0)
            with engine.Fori(1, ROUNDS // 2) as i:
                body(2 * i, 0, None)
                body(2 * i + 1, 1, None)
            body(ROUNDS, 0, None)

        def by_tile(engine, body):
            body(0, 0, 0)
            body(1, 1, 0)
            with engine.Fori(1, PER_TILE // 2) as i:
                body(2 * i, 0, None)
                body(2 * i + 1, 1, None)
            with engine.Fori(1, GATHER_TILES) as k:
                body(PER_TILE * k, 0, k)
                body(PER_TILE * k + 1, 1, k)
                with engine.Fori(1, PER_TILE // 2) as i:
                    body(PER_TILE * k + 2 * i, 0, None)
                    body(PER_TILE * k + 2 * i + 1, 1, None)
            body(ROUNDS, 0, None)

        def last(r):
            return isinstance(r, int) and r == ROUNDS

        def at_least(r, n):
            return not isinstance(r, int) or r >= n

        @block.sync
        def _(sp):
            sp.dma_start(h2T, scratch["h2T"]).then_inc(h2_in, 16)

            def load_u(n):
                sp.wait_ge(u_ready, n)
                sp.dma_start(u_raw[:, :, :], io["uT"][n]).then_inc(u_in, 16)

            load_u(0)
            load_u(1)

            def body(r, parity, _):
                if last(r):
                    return
                for e in range(PAIR):
                    n = 2 * r + e
                    sp.wait_ge(v_ready, n)
                    sp.dma_start(v_raw[:, :], io["v_rows"][:, n, :]).then_inc(v_in, 16)
                    sp.wait_ge(weighted, n)
                    sp.dma_start(g_raw[:, :], scratch["g"][n]).then_inc(g_in, 16)
                    load_u(n + 2)
            by_round(sp, body)
            sp.wait_ge(added, DENSE_TILES * (ROUNDS + 1))
            sp.dma_start(scratch["ffn"][0:DENSE_TILES].rearrange("t p n -> p t n"), acc[:, :, :]).then_inc(acc_out, 16)
            sp.wait_ge(acc_out, 16)

        @block.tensor
        def _(pe):
            pe.sem_inc(a_made, 2)
            pe.wait_ge(xT_ready, 1)

            def body(r, parity, _):
                if not last(r):
                    for e in range(PAIR):
                        n = 2 * r + e
                        pe.wait_ge(u_ready, n + 1)
                        pe.wait_ge(hidden_ready, n + 1)
                        for k in range(KD):
                            for part, xp in ((0, 0), (0, 1), (1, 0)):
                                for c in range(2):
                                    mm = nc.tensor.matmul(a_ps[e][:, c, 0:HALF], u[part][:, e, k, :],
                                                          xT[xp][:, k, c * HALF:(c + 1) * HALF],
                                                          start=(k == 0 and part == 0 and xp == 0),
                                                          stop=(k == KD - 1 and part == 1))
                        mm.then_inc(a_made, 1)
                if at_least(r, 1):
                    g = r - 1
                    pe.wait_ge(w_ready, 2 * g + 2 + 2)
                    pe.wait_ge(v_ready, 2 * g + 2)
                    for t in range(DENSE_TILES):
                        pe.wait_ge(added, DENSE_TILES * (g + 1) + t - 1)
                        for e in range(PAIR):
                            for part, xp in ((0, 0), (0, 1), (1, 0)):
                                for c in range(2):
                                    mm = nc.tensor.matmul(
                                        o_ps[t % 2][:, c, :], w[part][:, 1 - parity, e, t * P:(t + 1) * P],
                                        v[xp][:, 1 - parity, e, c * SLAB:(c + 1) * SLAB],
                                        start=(e == 0 and part == 0 and xp == 0), stop=(e == 1 and part == 1))
                        mm.then_inc(o_made, 1)
            by_round(pe, body)

        @block.scalar
        def _(act):
            act.sem_inc(hidden_ready, 2)

            def split_u(n, e):
                act.wait_ge(u_in, 16 * n + 16)
                act.wait_ge(a_made, n - 1 + 2)
                nc.scalar.activation(u[0][:, e, :, :], u_raw[:, :, :], ACT.Copy).then_inc(u_hi_ready, 1)

            split_u(0, 0)
            act.wait_ge(h2_in, 16)
            for k in range(KD):
                nc.scalar.activation(xT[0][:, k, :], h2T[:, k, :], ACT.Copy).then_inc(x_hi_ready, 1)
            split_u(1, 1)

            def body(r, parity, _):
                if last(r):
                    return
                for e in range(PAIR):
                    n = 2 * r + e
                    act.wait_ge(v_in, 16 * n + 16)
                    if at_least(r, 2):
                        act.wait_ge(o_made, DENSE_TILES * (r - 1))
                    nc.scalar.activation(v[0][:, parity, e, :], v_raw[:, :], ACT.Copy).then_inc(v_hi_ready, 1)
                    act.wait_ge(a_made, n + 1 + 2)
                    act.wait_ge(w_ready, n - 1 + 2)
                    nc.scalar.activation(hidden[:, e, :].rearrange("p (c n) -> p c n", c=2), a_ps[e][:, :, 0:HALF],
                                         ACT.Gelu).then_inc(hidden_ready, 1)
                    split_u(n + 2, e)
                    act.wait_ge(weighted, n + 1)
                    nc.scalar.activation(w[0][:, parity, e, :], hidden[:, e, :], ACT.Copy).then_inc(w_hi_ready, 1)
                act.wait_ge(dots, BATCH * (r + 1) + RING)
                nc.scalar.activation(gelu[:, parity, :], dot[:, parity, :], ACT.Gelu).then_inc(gelu_ready, 1)
            by_round(act, body)

        @block.gpsimd
        def _(pool):
            def stand(c):
                pool.sem_inc(passed, 1)

            def split(lo, raw, hi, hi_ready, ready, n):
                pool.wait_ge(hi_ready, n + 1)
                nc.gpsimd.tensor_tensor(lo, raw, f32(hi), ALU.subtract).then_inc(ready, 1)

            def split_u(n, e):
                split(u[1][:, e, :, :], u_raw[:, :, :], u[0][:, e, :, :], u_hi_ready, u_ready, n)

            def split_v(r, parity, e):
                split(v[1][:, parity, e, :], v_raw[:, :], v[0][:, parity, e, :], v_hi_ready, v_ready, 2 * r + e)

            split_u(0, 0)
            split_u(1, 1)

            def body(r, parity, tile):
                c = Chain(pool, own_pool)
                if tile is not None and not last(r) and parity == 0:
                    pool.wait_ge(dots, BATCH * r + RING)
                    stand(c)
                    pool.dma_start(x[:, :], scratch["h2"][tile]).then_inc(x_in, 16)
                if tile is not None and parity == 1 and not isinstance(tile, int):
                    pool.wait_ge(summed, BATCH * (r - 1) + RING)
                    stand(c)
                    pool.dma_start(scratch["ffn"][tile + (DENSE_TILES - 1)], total[:, :]).then_inc(total_out, 16)
                if not last(r):
                    c.step(nc.gpsimd.tensor_copy(u_id[:, parity, :], expert_id[:, bass.ds(BATCH * r, BATCH)]))
                if at_least(r, 1):
                    c.step(nc.gpsimd.tensor_copy(v_id[:, parity, :], expert_id[:, bass.ds(BATCH * (r - 1), BATCH)]))
                c.wait()
                for j in range(BATCH):
                    if not last(r):
                        pool.wait_ge(dots, BATCH * r + j + 1)
                    if at_least(r, 1):
                        pool.wait_ge(summed, BATCH * (r - 1) + j + 1)
                    stand(c)
                    if not last(r):
                        nc.gpsimd.indirect_dma_start(
                            out=u_row[:, j % RING, :], out_offset=None, in_=io["u_rows"],
                            in_offset=bass.IndirectOffsetOnAxis(ap=u_id[:, parity, j:j + 1], axis=0))\
                          .then_inc(u_row_in[j % RING], 16)
                    if at_least(r, 1):
                        nc.gpsimd.indirect_dma_start(
                            out=v_row[:, j % RING, :], out_offset=None, in_=io["v_rows"].rearrange("a b n -> (a b) n"),
                            in_offset=bass.IndirectOffsetOnAxis(ap=v_id[:, parity, j:j + 1], axis=0))\
                          .then_inc(v_row_in[j % RING], 16)
                    if not last(r):
                        if j == 1 and at_least(r, 1):
                            split_u(2 * r + 1, 1)
                        if j == 4:
                            split_v(r, parity, 0)
                        if j == 6:
                            split_u(2 * r + 2, 0)
                        if j == 7:
                            split_v(r, parity, 1)
                c.reset()
            by_tile(pool, body)
            pool.wait_ge(summed, BATCH * ROUNDS + RING)
            pool.dma_start(scratch["ffn"][TILES - 1], total[:, :]).then_inc(total_out, 16)
            pool.wait_ge(total_out, 16 * GATHER_TILES)

        @block.vector
        def _(dve):
            dve.sem_inc(w_ready, 2)
            dve.sem_inc(added, DENSE_TILES)
            dve.sem_inc(dots, RING)
            dve.sem_inc(summed, RING)
            for k in range(KD):
                dve.wait_ge(x_hi_ready, k + 1)
                lo = nc.vector.tensor_tensor(xT[1][:, k, :], h2T[:, k, :], f32(xT[0][:, k, :]), ALU.subtract)
            lo.then_inc(xT_ready, 1)
            dve.wait_ge(xT_ready, 1)
            nc.vector.memset(acc[:, :, :], 0.0).then_inc(zeroed, 1)
            dve.wait_ge(zeroed, 1)

            def body(r, parity, tile):
                def dot_product(j):
                    if last(r):
                        return
                    if j == 0 and tile is not None and parity == 0:
                        dve.wait_ge(x_in, 16 * tile + 16)
                    dve.wait_ge(u_row_in[j % RING], 32 * r + 16 * (j // RING) + 16)
                    nc.vector.tensor_tensor_reduce(out=u_row[:, j % RING, :], in0=u_row[:, j % RING, :], in1=x[:, :],
                                                   scale=1.0, scalar=0.0, op0=ALU.mult, op1=ALU.add,
                                                   accum_out=dot[:, parity, j:j + 1]).then_inc(dots, 1)

                def factors():
                    if at_least(r, 1):
                        dve.wait_ge(gelu_ready, r)
                        nc.vector.tensor_tensor(factor[:, 1 - parity, :], gelu[:, 1 - parity, :],
                                                share[:, bass.ds(BATCH * (r - 1), BATCH)], ALU.mult)\
                          .then_inc(factor_ready, 1)
                        dve.wait_ge(factor_ready, r)

                def add_row(j):
                    if not at_least(r, 1):
                        return
                    row, by = v_row[:, j % RING, :], factor[:, 1 - parity, j:j + 1]
                    dve.wait_ge(v_row_in[j % RING], 32 * (r - 1) + 16 * (j // RING) + 16)
                    if j == 0 and parity == 1 and tile is not None:
                        dve.wait_ge(total_out, 16 * tile)
                        dve.wait_ge(summed, BATCH * (r - 1) + RING)
                        nc.vector.tensor_scalar(total[:, :], row, by, None, ALU.mult).then_inc(summed, 1)
                    else:
                        dve.wait_ge(summed, BATCH * (r - 1) + j + RING)
                        nc.vector.scalar_tensor_tensor(total[:, :], row, by, total[:, :], ALU.mult, ALU.add)\
                          .then_inc(summed, 1)

                def weigh(e):
                    if not last(r):
                        n = 2 * r + e
                        dve.wait_ge(g_in, 16 * n + 16)
                        dve.wait_ge(hidden_ready, n + 1 + 2)
                        nc.vector.tensor_tensor(hidden[:, e, :], hidden[:, e, :], g_raw[:, :], ALU.mult)\
                          .then_inc(weighted, 1)

                def split_w(e):
                    if not last(r):
                        dve.wait_ge(w_hi_ready, 2 * r + e + 1)
                        nc.vector.tensor_tensor(w[1][:, parity, e, :], hidden[:, e, :], f32(w[0][:, parity, e, :]),
                                                ALU.subtract).then_inc(w_ready, 1)

                def add_tile(back, t):
                    if at_least(r, back):
                        g = r - back
                        dve.wait_ge(o_made, DENSE_TILES * g + t + 1)
                        dve.wait_ge(added, DENSE_TILES * g + t + 1)
                        nc.vector.tensor_tensor(acc[:, t, :], o_ps[t % 2][:, :, :].rearrange("p c n -> p (c n)"),
                                                acc[:, t, :], ALU.add).then_inc(added, 1)

                D, X = dot_product, add_row
                D(0); factors(); X(0); add_tile(2, DENSE_TILES - 2)
                D(1); X(1); add_tile(2, DENSE_TILES - 1)
                D(2); X(2); D(3)
                weigh(0)
                X(3); D(4)
                split_w(0)
                X(4); D(5)
                weigh(1)
                X(5); add_tile(1, 0)
                split_w(1)
                D(6); add_tile(1, 1); X(6); add_tile(1, 2); D(7); add_tile(1, 3); X(7)
                if last(r):
                    add_tile(1, DENSE_TILES - 2)
                    add_tile(1, DENSE_TILES - 1)
            by_tile(dve, body)


def final_norm(nc, io, scratch):
    PAIRS = TILES // 2
    with Scope(nc, "last") as s:
        norm_w = s.sb("norm_w", [P, D])
        gate = s.sb("gate", [P, 2, D])
        x1 = s.sb("x1", [P, TILES, D])
        f = s.sb("f", [P, TILES, D])
        y = s.sb("y", [P, 2, D])
        square = s.sb("square", [P, D])
        total = s.sb("total", [P, TILES])
        rstd = s.sb("rstd", [P, TILES])
        eps = s.sb("eps", [P, 1])
        w_in = s.sem("w_in")
        pair_in = [s.sem(f"pair_in{n}") for n in range(PAIRS)]
        y_out = [s.sem(f"y_out{n}") for n in range(2)]
        eps_ready = s.sem("eps_ready")
        gated = s.sem("gated")
        x2_ready = s.sem("x2_ready")
        summed = s.sem("summed")
        root_ready = s.sem("root_ready")
        rstd_ready = s.sem("rstd_ready")
        y_ready = s.sem("y_ready")
        block = s.block()

        @block.sync
        def _(sp):
            sp.dma_start(gate[:, :, :], scratch["gate"]).then_inc(w_in, 16)
            sp.dma_start(norm_w[:, :], io["norm_f"].partition_broadcast(P)).then_inc(w_in, 16)
            for i in range(PAIRS):
                for source, out in (("ffn", f), ("x1", x1)):
                    sp.dma_start(out[:, 2 * i:2 * i + 2, :], scratch[source][2 * i:2 * i + 2].rearrange("t p n -> p t n"))\
                      .then_inc(pair_in[i], 16)
            for t in range(TILES):
                sp.wait_ge(y_ready, t + 1)
                sp.dma_start(io["y"][t * P:(t + 1) * P, :], y[:, t % 2, :]).then_inc(y_out[t % 2], 16)
            for j in range(2):
                sp.wait_ge(y_out[j], 16 * PAIRS)

        @block.scalar
        def _(act):
            act.wait_ge(eps_ready, 1)
            for i in range(PAIRS):
                for t in (2 * i, 2 * i + 1):
                    act.wait_ge(x2_ready, t + 1)
                    nc.scalar.activation(square[:, :], f[:, t, :], ACT.Square, accum_out=total[:, t:t + 1])\
                      .then_inc(summed, 1)
                    act.wait_ge(summed, t + 1)
                nc.scalar.activation(total[:, 2 * i:2 * i + 2], total[:, 2 * i:2 * i + 2], ACT.Sqrt, scale=1.0 / D,
                                     bias=eps[:, 0:1]).then_inc(root_ready, 1)

        @block.vector
        def _(dve):
            nc.vector.memset(eps[:, :], EPS).then_inc(eps_ready, 1)
            dve.wait_ge(w_in, 32)

            def residual(i):
                dve.wait_ge(pair_in[i], 32)
                for t in (2 * i, 2 * i + 1):
                    cnd = LATENT_COND if t < LATENT_TILES else CONTEXT_COND
                    nc.vector.tensor_tensor(f[:, t, :], f[:, t, :], gate[:, cnd, :], ALU.mult).then_inc(gated, 1)
                    dve.wait_ge(gated, t + 1)
                    nc.vector.tensor_tensor(f[:, t, :], f[:, t, :], x1[:, t, :], ALU.add).then_inc(x2_ready, 1)

            residual(0)
            for i in range(PAIRS):
                if i + 1 < PAIRS:
                    residual(i + 1)
                dve.wait_ge(root_ready, i + 1)
                nc.vector.reciprocal(rstd[:, 2 * i:2 * i + 2], total[:, 2 * i:2 * i + 2]).then_inc(rstd_ready, 1)
                dve.wait_ge(rstd_ready, i + 1)
                for t in (2 * i, 2 * i + 1):
                    if i:
                        dve.wait_ge(y_out[t % 2], 16 * i)
                    nc.vector.scalar_tensor_tensor(y[:, t % 2, :], f[:, t, :], rstd[:, t:t + 1], norm_w[:, :],
                                                   ALU.mult, ALU.mult).then_inc(y_ready, 1)


def program(nc, io):
    scratch = {name: nc.dram_tensor(f"scratch_{name}", shape, FP32).ap() for name, shape in SCRATCH.items()}
    with Scope(nc, "keep") as s:
        keep = {
            "ident": s.sb("ident", [P, P]),
            "iota": s.sb("iota", [P, P]),
            "mod_cols": s.sb("mod_cols", [P, 6, KD, 2]),
            "factor": s.sb("factor", [P, 2, KD, 2]),
            "silu": s.sb("silu", [P, KD, 2]),
            "b_mod": s.sb("b_mod", [P, 6, KD]),
            "norm_col": s.sb("norm_col", [P, 2, KD]),
        }
        constants_and_modulation(nc, io, keep)
        expert_id = s.sb("expert_id", [P, GATHER_TILES * SLOTS], I32)
        share = s.sb("share", [P, GATHER_TILES * SLOTS])
        with Scope(nc, "mix") as m:
            featT = m.sb("featT", [P, KD, T])
            with Scope(nc, "heads") as h:
                fused = h.sb("fused", [P, K0 + 4, T])
                v = h.sb("v", [P, TILES, SLAB])
                input_norm(nc, io, keep, featT)
                projection_and_rg_lru(nc, io, keep, featT, fused, v)
                attention(nc, io, keep, fused, v, featT)
            out_projection(nc, io, keep, featT, scratch)
            with Scope(nc, "routes") as q:
                first = q.sb("first", [P, TILES * PEER_HEADS // 2, 2 * TOPK])
                second = q.sb("second", [P, TILES * PEER_HEADS // 2, 2 * TOPK])
                weight = q.sb("weight", [P, TILES * PEER_HEADS // 2, 2 * TOPK])
                routing(nc, io, keep, featT, scratch, first, second, weight, expert_id, share)
                place_weights(nc, io, keep, scratch, first, second, weight, DENSE_TILES)
        experts(nc, io, scratch, expert_id, share)
        final_norm(nc, io, scratch)


def kernel(**inputs):
    from concourse import bacc
    from concourse.bass_utils import run_bass_kernel_spmd

    nc = bacc.Bacc("TRN2", target_bir_lowering=False, num_devices=1)
    arrays, io = laid_out(inputs), {}
    for name, a in arrays.items():
        io[name] = nc.dram_tensor(f"in_{name}", a.shape, mybir.dt.from_np(a.dtype), kind="ExternalInput").ap()
    for name, shape in OUTPUTS.items():
        io[name] = nc.dram_tensor(f"out_{name}", shape, FP32, kind="ExternalOutput").ap()
    program(nc, io)
    r = run_bass_kernel_spmd(nc, [{f"in_{k}": a for k, a in arrays.items()}], core_ids=[0]).results[0]
    return (r["out_y"][LATENT:].reshape(1, CONTEXT, D), r["out_y"][:LATENT].reshape(1, LATENT, D),
            r["out_new_k"].reshape(1, 1, CONTEXT, HEADS, HD), r["out_new_v"].reshape(1, 1, CONTEXT, HEADS, HD),
            r["out_new_state"].transpose(1, 2, 0).reshape(1, 1, 2, 512))


OUTPUTS = {"y": (T, D), "new_k": (CONTEXT, 512), "new_v": (CONTEXT, 512), "new_state": (P, 2, RG_TILES)}


SCRATCH = {"x1": (TILES, P, D), "h2T": (P, KD, DENSE_TILES * P), "g": (N_KEYS, P, DENSE_TILES * P), "h2": (GATHER_TILES, P, D), "gate": (P, 2, D), "ffn": (TILES, P, D)}


def laid_out(inputs):
    a = {k: np.asarray(x) for k, x in inputs.items()}

    def columns(rows):
        rows = np.atleast_2d(rows)
        return np.ascontiguousarray(rows.reshape(rows.shape[0], -1, P).transpose(2, 0, 1))

    w_in = a["w_in"][0].reshape(D, 5, 512)
    blocks = np.zeros((RG_TILES, P, 4, P), np.float32)
    for n, w in enumerate((a["rg_w_a"][0, 0], a["rg_w_i"][0, 0], a["rg_w_a"][0, 1], a["rg_w_i"][0, 1])):
        for b in range(8):
            at = 64 * (b % 2)
            blocks[b // 2, at:at + 64, n, at:at + 64] = w[b]
    rpb = np.pad(a["rpb"][0], ((0, 0), (0, 0), (48, 48)))
    q_col = np.arange(GRID_W)[:, None]
    k_col = np.arange(GRID_W)[None, :]
    toeplitz = rpb[:, :, k_col - q_col + GRID_W - 1]
    out = {
        "x": np.concatenate([a["x_sample"][0], a["x_prompt"][0]]).reshape(TILES, P, D),
        "cond": np.ascontiguousarray(columns(np.stack([a["c"][0], a["c_ctx"]])).transpose(0, 2, 1)),
        "w_mod": a["w_mod"][0],
        "b_mod_cols": columns(a["b_mod"][0].reshape(6, D)),
        "norm_cols": columns(np.stack([a["norm_mix_w"][0], a["norm_ffn_w"][0]])),
        "norm_f": a["norm_f_w"],
        "w_in": np.ascontiguousarray(w_in[:, [3, 4, 0, 1, 2]].reshape(D, -1)),
        "rel_bias": np.ascontiguousarray(toeplitz.transpose(2, 0, 1, 3)),
        "k_ctxT": np.ascontiguousarray(a["cache_k"][0, 0].reshape(PAST, 4, P).transpose(2, 1, 0)),
        "v_ctx": a["cache_v"][0, 0].reshape(2, P, 512),
        "rg_blocks": blocks,
        "rg_cols": columns(np.concatenate([a["conv_w"][0], a["conv_b"], a["rg_b_a"][0], a["rg_b_i"][0],
                                           a["rg_lambda"][0], a["state_rglru"][0, 0]])),
        "w_out": a["w_out"][0],
        "w_q": a["peer_w_q"][0],
        "keysT": np.ascontiguousarray(a["peer_sub_keys"][0].transpose(2, 0, 1)),
        "uT": np.concatenate([a["peer_u"][0].reshape(N_KEYS, N_KEYS, KD, P).transpose(1, 3, 2, 0),
                              np.zeros((2, P, KD, P), np.float32)]),
        "u_rows": a["peer_u"][0],
        "v_rows": a["peer_v"][0].reshape(N_KEYS, N_KEYS, D),
    }
    return {k: np.ascontiguousarray(x) for k, x in out.items()}
```
